# Optimizing a Trainium2 kernel written in Bass

```python
import jax, jax.numpy as jnp
from jax import lax
import numpy as np
import math

D_MODEL = 1024
BATCH = 1
SEQ = 512
DEPTH = 1

D_MIX = D_MODEL
D_LRU = D_MIX // 2
D_CONV = D_MIX - D_LRU
LRU_HEADS = 8
LRU_HEAD_DIM = D_LRU // LRU_HEADS
LRU_CONV_WIDTH = 4
LRU_C = 8.0
LRU_A_MIN = 0.9
LRU_A_MAX = 0.999
CONV_GROUPS = 8
CONV_GROUP_DIM = D_CONV // CONV_GROUPS
CONF_KERNEL = 31
PEER_HEADS = 8
PEER_N_KEYS = 128
PEER_N_EXPERTS = PEER_N_KEYS ** 2
PEER_D_QUERY = 256
PEER_HALF = PEER_D_QUERY // 2
PEER_TOPK = 16
PEER_BLOCK = 128
EPS = 1e-6


def rms_norm(x, g):
    xf = x.astype(jnp.float32)
    y = xf * lax.rsqrt(jnp.mean(xf * xf, axis=-1, keepdims=True) + EPS)
    return (y * g.astype(jnp.float32)).astype(x.dtype)

def group_layer_norm(x, g, b):
    B_, S_, C = x.shape
    xg = x.astype(jnp.float32).reshape(B_, S_, CONV_GROUPS, CONV_GROUP_DIM)
    mu = jnp.mean(xg, axis=-1, keepdims=True)
    var = jnp.mean(jnp.square(xg - mu), axis=-1, keepdims=True)
    y = ((xg - mu) * lax.rsqrt(var + EPS)).reshape(B_, S_, C)
    return (y * g.astype(jnp.float32) + b.astype(jnp.float32)).astype(x.dtype)

def depthwise_conv(x, w, b, pad):
    C = x.shape[-1]
    y = lax.conv_general_dilated(
        x, w[:, None, :].astype(x.dtype), window_strides=(1,), padding=[pad],
        dimension_numbers=("NWC", "WIO", "NWC"), feature_group_count=C)
    return y + b.astype(x.dtype)

def block_diag_linear(x, w, b):
    B_, S_, _ = x.shape
    xh = x.reshape(B_, S_, LRU_HEADS, LRU_HEAD_DIM)
    y = jnp.einsum("bshi,hij->bshj", xh, w.astype(jnp.float32))
    return y.reshape(B_, S_, D_LRU) + b.astype(jnp.float32)

def _linear_recurrence(left, right):
    a_l, b_l = left
    a_r, b_r = right
    return a_l * a_r, a_r * b_l + b_r

def rg_lru(x, w_r, b_r, w_i, b_i, lam, reverse):
    xf = x.astype(jnp.float32)
    r = jax.nn.sigmoid(block_diag_linear(xf, w_r, b_r))
    i = jax.nn.sigmoid(block_diag_linear(xf, w_i, b_i))
    log_a = LRU_C * r * jax.nn.log_sigmoid(lam.astype(jnp.float32))
    a = jnp.exp(log_a)
    u = jnp.sqrt(-jnp.expm1(2.0 * log_a)) * (i * xf)
    _, h = lax.associative_scan(_linear_recurrence, (a, u), reverse=reverse, axis=1)
    return h

def hybrid_mixer(n, w_in, lru_conv_w, lru_conv_b, lru_w_rg, lru_b_rg, lru_w_ig, lru_b_ig,
                 lru_lambda, conf_conv_w, conf_conv_b, conf_norm_g, conf_norm_b,
                 beta_lru, beta_conv, w_out):
    z = jnp.einsum("bsd,de->bse", n, w_in.astype(n.dtype))
    x_lru, g_lru, a_glu, b_glu = jnp.split(
        z, [D_LRU, 2 * D_LRU, 2 * D_LRU + D_CONV], axis=-1)

    lpad = LRU_CONV_WIDTH // 2
    xc = depthwise_conv(x_lru, lru_conv_w, lru_conv_b, (lpad, LRU_CONV_WIDTH - 1 - lpad))
    h_fwd = rg_lru(xc, lru_w_rg[0], lru_b_rg[0], lru_w_ig[0], lru_b_ig[0], lru_lambda[0], False)
    h_bwd = rg_lru(xc, lru_w_rg[1], lru_b_rg[1], lru_w_ig[1], lru_b_ig[1], lru_lambda[1], True)
    y_lru = ((h_fwd + h_bwd) * jax.nn.gelu(g_lru.astype(jnp.float32))).astype(n.dtype)

    glu = a_glu * jax.nn.sigmoid(b_glu)
    c = depthwise_conv(glu, conf_conv_w, conf_conv_b, (CONF_KERNEL // 2, CONF_KERNEL // 2))
    y_conv = jax.nn.silu(group_layer_norm(c, conf_norm_g, conf_norm_b))

    y = jnp.concatenate([rms_norm(y_lru, beta_lru), rms_norm(y_conv, beta_conv)], axis=-1)
    return jnp.einsum("bse,ed->bsd", y, w_out.astype(y.dtype))

def peer_ffn(n, w_q, sub_keys, expert_u, expert_v):
    B_, S_, D = n.shape
    n_blocks = (B_ * S_) // PEER_BLOCK
    xb = n.reshape(n_blocks, PEER_BLOCK, D)

    def retrieve(xt):
        q = jnp.einsum("td,de->te", xt, w_q.astype(xt.dtype))
        q = q.reshape(PEER_BLOCK, PEER_HEADS, 2, PEER_HALF).astype(jnp.float32)
        s = jnp.einsum("thpc,hpkc->thpk", q, sub_keys.astype(jnp.float32))
        s1, i1 = lax.top_k(s[:, :, 0], PEER_TOPK)
        s2, i2 = lax.top_k(s[:, :, 1], PEER_TOPK)
        cand_s = (s1[..., :, None] + s2[..., None, :]).reshape(PEER_BLOCK, PEER_HEADS, PEER_TOPK * PEER_TOPK)
        cand_i = (i1[..., :, None] * PEER_N_KEYS + i2[..., None, :]).reshape(PEER_BLOCK, PEER_HEADS, PEER_TOPK * PEER_TOPK)
        top_s, pos = lax.top_k(cand_s, PEER_TOPK)
        idx = jnp.take_along_axis(cand_i, pos, axis=-1)
        gate = jax.nn.softmax(top_s, axis=-1)
        u = expert_u[idx]
        v = expert_v[idx]
        act = jax.nn.gelu(jnp.einsum("thkd,td->thk", u, xt))
        return jnp.einsum("thk,thkd->td", (gate * act).astype(v.dtype), v)

    out = lax.map(retrieve, xb)
    return out.reshape(B_, S_, D).astype(n.dtype)

def first_inputs(seed: int = 0) -> dict:
    key = jax.random.key(seed)
    ks = jax.random.split(key, 24)
    L = DEPTH
    nrm = lambda k, shape, scale: jax.random.normal(k, shape, jnp.float32) * scale
    gain = lambda k, shape: 1.0 + 0.02 * jax.random.normal(k, shape, jnp.float32)
    a0 = jax.random.uniform(ks[9], (L, 2, D_LRU), jnp.float32, LRU_A_MIN, LRU_A_MAX)
    p = a0 ** (1.0 / LRU_C)
    lru_lambda = jnp.log(p) - jnp.log1p(-p)
    return {
        "x": nrm(ks[0], (BATCH, SEQ, D_MODEL), 1.0),
        "mix_norm_g": gain(ks[1], (L, D_MODEL)),
        "w_in": nrm(ks[2], (L, D_MODEL, 2 * D_LRU + 2 * D_CONV), D_MODEL ** -0.5),
        "lru_conv_w": nrm(ks[3], (L, LRU_CONV_WIDTH, D_LRU), LRU_CONV_WIDTH ** -0.5),
        "lru_conv_b": nrm(ks[4], (L, D_LRU), 0.02),
        "lru_w_rg": nrm(ks[5], (L, 2, LRU_HEADS, LRU_HEAD_DIM, LRU_HEAD_DIM), LRU_HEAD_DIM ** -0.5),
        "lru_b_rg": nrm(ks[6], (L, 2, D_LRU), 0.02),
        "lru_w_ig": nrm(ks[7], (L, 2, LRU_HEADS, LRU_HEAD_DIM, LRU_HEAD_DIM), LRU_HEAD_DIM ** -0.5),
        "lru_b_ig": nrm(ks[8], (L, 2, D_LRU), 0.02),
        "lru_lambda": lru_lambda,
        "conf_conv_w": nrm(ks[10], (L, CONF_KERNEL, D_CONV), CONF_KERNEL ** -0.5),
        "conf_conv_b": nrm(ks[11], (L, D_CONV), 0.02),
        "conf_norm_g": gain(ks[12], (L, D_CONV)),
        "conf_norm_b": nrm(ks[13], (L, D_CONV), 0.02),
        "beta_lru": gain(ks[14], (L, D_LRU)),
        "beta_conv": gain(ks[15], (L, D_CONV)),
        "w_out": nrm(ks[16], (L, D_MIX, D_MODEL), D_MIX ** -0.5),
        "ffn_norm_g": gain(ks[17], (L, D_MODEL)),
        "peer_w_q": nrm(ks[18], (L, D_MODEL, PEER_HEADS * PEER_D_QUERY), D_MODEL ** -0.5),
        "peer_sub_keys": nrm(ks[19], (L, PEER_HEADS, 2, PEER_N_KEYS, PEER_HALF), PEER_HALF ** -0.5),
        "peer_u": nrm(ks[20], (L, PEER_N_EXPERTS, D_MODEL), D_MODEL ** -0.5),
        "peer_v": nrm(ks[21], (L, PEER_N_EXPERTS, D_MODEL), PEER_HEADS ** -0.5),
        "final_norm_g": gain(ks[22], (D_MODEL,)),
    }

def first_block(x, mix_norm_g, w_in, lru_conv_w, lru_conv_b, lru_w_rg, lru_b_rg, lru_w_ig,
              lru_b_ig, lru_lambda, conf_conv_w, conf_conv_b, conf_norm_g, conf_norm_b,
              beta_lru, beta_conv, w_out, ffn_norm_g, peer_w_q, peer_sub_keys, peer_u,
              peer_v, final_norm_g):
    h = x
    for l in range(DEPTH):
        h = h + hybrid_mixer(
            rms_norm(h, mix_norm_g[l]), w_in[l], lru_conv_w[l], lru_conv_b[l],
            lru_w_rg[l], lru_b_rg[l], lru_w_ig[l], lru_b_ig[l], lru_lambda[l],
            conf_conv_w[l], conf_conv_b[l], conf_norm_g[l], conf_norm_b[l],
            beta_lru[l], beta_conv[l], w_out[l])
        h = h + peer_ffn(rms_norm(h, ffn_norm_g[l]), peer_w_q[l], peer_sub_keys[l],
                         peer_u[l], peer_v[l])
    return rms_norm(h, final_norm_g)


DEPTH_2 = 2

N_A_LAYERS = (DEPTH_2 + 1) // 2
N_B_LAYERS = DEPTH_2 - N_A_LAYERS
HEAD_DIM = 64
N_HEADS = D_MODEL // HEAD_DIM
N_KV = 4
GQA_R = N_HEADS // N_KV
KV_DIM = N_KV * HEAD_DIM
NUM_BUCKETS = 32
MAX_DISTANCE = 2048
CMP_BLOCK = 32
CMP_STRIDE = 16
CMP_HIDDEN = 256
SEL_BLOCK = 64
SEL_TOPN = 8
SEL_Q_CHUNK = 16
FORCE_BONUS = 100.0
WIN = 256
BAND_BLOCK = 128
DILATIONS = ((128, 1), (512, 4), (2048, 16))
N_DIL = len(DILATIONS)
FFN_HIDDEN = -(-8 * D_MODEL // (3 * 256)) * 256
RMS_EPS = 1e-6
NEG_INF = -1e30
A_IN_DIM = D_MODEL + 6 * KV_DIM + 3 * N_HEADS
B_Q_DIM = N_DIL * D_MODEL
SHARED_KV_DIM = N_DIL * 2 * KV_DIM


def rmsnorm(x, g):
    x32 = x.astype(jnp.float32)
    y = x32 * lax.rsqrt(jnp.mean(x32 * x32, axis=-1, keepdims=True) + RMS_EPS)
    return (y * g.astype(jnp.float32)).astype(x.dtype)

def t5_bucket(dist):
    max_exact = NUM_BUCKETS // 2
    d = jnp.maximum(dist, 0)
    log_ratio = jnp.log(jnp.maximum(d, max_exact).astype(jnp.float32) / max_exact) / math.log(MAX_DISTANCE / max_exact)
    large = max_exact + (log_ratio * (NUM_BUCKETS - max_exact)).astype(jnp.int32)
    return jnp.where(d < max_exact, d, jnp.minimum(large, NUM_BUCKETS - 1))

def masked_softmax(s, mask):
    s = jnp.where(mask, s.astype(jnp.float32), NEG_INF)
    m = jnp.max(s, axis=-1, keepdims=True)
    p = jnp.where(mask, jnp.exp(s - m), 0.0)
    return p, jnp.sum(p, axis=-1, keepdims=True), m

def banded_attention(q, k, v, max_dist, dist_scale, rel_bias):
    n, L, G, R, dh = q.shape
    nb = L // BAND_BLOCK
    n_prev = -(-max_dist // BAND_BLOCK)
    pad = n_prev * BAND_BLOCK
    kw_len = (n_prev + 1) * BAND_BLOCK

    def windows(t):
        tp = jnp.pad(t, ((0, 0), (pad, 0), (0, 0), (0, 0))).reshape(n, nb + n_prev, BAND_BLOCK, G, dh)
        return jnp.concatenate([tp[:, j:j + nb] for j in range(n_prev + 1)], axis=2)

    kw, vw = windows(k), windows(v)
    qb = q.reshape(n, nb, BAND_BLOCK, G, R, dh)
    s = jnp.einsum('nbqgrd,nbkgd->nbgrqk', qb, kw).astype(jnp.float32) * dh ** -0.5
    qi = jnp.arange(BAND_BLOCK)[:, None]
    ki = jnp.arange(kw_len)[None, :]
    dist = pad + qi - ki
    key_pos = jnp.arange(nb)[:, None, None] * BAND_BLOCK - pad + ki[None]
    mask = (dist >= 0) & (dist <= max_dist) & (key_pos >= 0)
    bias = rel_bias[t5_bucket(dist * dist_scale)].reshape(BAND_BLOCK, kw_len, G, R).transpose(2, 3, 0, 1)
    p, denom, m = masked_softmax(s + bias, mask[None, :, None, None])
    o = jnp.einsum('nbgrqk,nbkgd->nbqgrd', p, vw.astype(jnp.float32))
    o = o / denom[..., 0].transpose(0, 1, 4, 2, 3)[..., None]
    lse = (jnp.log(denom) + m)[..., 0].transpose(0, 1, 4, 2, 3).reshape(n, L, G, R)
    return o.reshape(n, L, G, R, dh), lse

def dilated_group_attention(q, k, v, dilation, window, rel_bias):
    B, S = q.shape[:2]
    L = S // dilation
    Lp = -(-L // BAND_BLOCK) * BAND_BLOCK

    def to_sub(t):
        rest = t.shape[2:]
        t = t.reshape((B, L, dilation) + rest)
        t = jnp.moveaxis(t, 2, 1).reshape((B * dilation, L) + rest)
        return jnp.pad(t, ((0, 0), (0, Lp - L)) + ((0, 0),) * len(rest))

    def from_sub(t):
        rest = t.shape[2:]
        t = t[:, :L].reshape((B, dilation, L) + rest)
        return jnp.moveaxis(t, 1, 2).reshape((B, S) + rest)

    o, lse = banded_attention(to_sub(q), to_sub(k), to_sub(v), window // dilation, dilation, rel_bias)
    return from_sub(o), from_sub(lse)

def nsa_attention(h, w_in, b_gate, pe_k, w1_k, w2_k, pe_v, w1_v, w2_v, w_out, rel_bias):
    B, S, _ = h.shape
    proj = h @ w_in
    splits = [D_MODEL + i * KV_DIM for i in range(7)]
    q, kc, vc, ks, vs, kwn, vwn, gl = jnp.split(proj, splits, axis=-1)
    q = q.reshape(B, S, N_KV, GQA_R, HEAD_DIM)
    kvh = lambda t: t.reshape(B, S, N_KV, HEAD_DIM)
    scale = HEAD_DIM ** -0.5
    t_pos = jnp.arange(S)

    n_c = (S - CMP_BLOCK) // CMP_STRIDE + 1
    starts = jnp.arange(n_c) * CMP_STRIDE
    tok_idx = starts[:, None] + jnp.arange(CMP_BLOCK)[None, :]

    def compress(t, pe, w1, w2):
        blk = t[:, tok_idx] + pe[:, None, :]
        blk = jnp.moveaxis(blk, 3, 2).reshape(B, n_c, N_KV, CMP_BLOCK * HEAD_DIM)
        return jax.nn.gelu(blk @ w1) @ w2

    k_cmp = compress(kvh(kc), pe_k, w1_k, w2_k)
    v_cmp = compress(kvh(vc), pe_v, w1_v, w2_v)
    dist_c = t_pos[:, None] - (starts + CMP_BLOCK - 1)[None, :]
    bias_c = rel_bias[t5_bucket(dist_c)].reshape(S, n_c, N_KV, GQA_R).transpose(2, 3, 0, 1)
    s = jnp.einsum('bsgrd,bngd->bgrsn', q, k_cmp).astype(jnp.float32) * scale
    p, denom, _ = masked_softmax(s + bias_c, dist_c >= 0)
    p_cmp = p / jnp.maximum(denom, 1e-30)
    o_cmp = jnp.einsum('bgrsn,bngd->bsgrd', p_cmp, v_cmp.astype(jnp.float32))

    n_sel = S // SEL_BLOCK
    top_n = min(SEL_TOPN, n_sel)
    ci = jnp.arange(n_c)[:, None] * CMP_STRIDE
    sj = jnp.arange(n_sel)[None, :] * SEL_BLOCK
    overlap = ((ci < sj + SEL_BLOCK) & (ci + CMP_BLOCK > sj)).astype(jnp.float32)
    imp = jnp.einsum('bgrsn,nj->bgsj', p_cmp, overlap)
    blk_j = jnp.arange(n_sel)[None, :]
    cur = (t_pos // SEL_BLOCK)[:, None]
    forced = (blk_j == 0) | (blk_j == cur) | (blk_j == cur - 1)
    score = jnp.where(forced, imp + FORCE_BONUS, jnp.where(blk_j <= cur, imp, -1.0))
    _, sel_idx = lax.top_k(score, top_n)

    k_blocks = kvh(ks).reshape(B, n_sel, SEL_BLOCK, N_KV, HEAD_DIM).transpose(0, 3, 1, 2, 4)
    v_blocks = kvh(vs).reshape(B, n_sel, SEL_BLOCK, N_KV, HEAD_DIM).transpose(0, 3, 1, 2, 4)
    n_chunk = S // SEL_Q_CHUNK
    q_ch = jnp.moveaxis(q.reshape(B, n_chunk, SEL_Q_CHUNK, N_KV, GQA_R, HEAD_DIM), 1, 0)
    idx_ch = jnp.moveaxis(sel_idx.reshape(B, N_KV, n_chunk, SEL_Q_CHUNK, top_n), 2, 0)
    c0 = jnp.arange(n_chunk) * SEL_Q_CHUNK
    b_ix = jnp.arange(B)[:, None, None, None]
    g_ix = jnp.arange(N_KV)[None, :, None, None]
    rb_g = rel_bias.reshape(NUM_BUCKETS, N_KV, GQA_R).transpose(1, 0, 2)
    n_keys = top_n * SEL_BLOCK

    def sel_chunk(args):
        qc, ic, start = args
        kg = k_blocks[b_ix, g_ix, ic].reshape(B, N_KV, SEL_Q_CHUNK, n_keys, HEAD_DIM)
        vg = v_blocks[b_ix, g_ix, ic].reshape(B, N_KV, SEL_Q_CHUNK, n_keys, HEAD_DIM)
        kpos = (ic[..., None] * SEL_BLOCK + jnp.arange(SEL_BLOCK)).reshape(B, N_KV, SEL_Q_CHUNK, n_keys)
        dist = (start + jnp.arange(SEL_Q_CHUNK))[:, None] - kpos
        bias = jnp.moveaxis(rb_g[g_ix, t5_bucket(dist)], -1, 3)
        s_sel = jnp.einsum('bcgrd,bgckd->bgcrk', qc, kg).astype(jnp.float32) * scale + bias
        p_sel, den, _ = masked_softmax(s_sel, (dist >= 0)[:, :, :, None, :])
        return jnp.einsum('bgcrk,bgckd->bcgrd', p_sel / jnp.maximum(den, 1e-30), vg.astype(jnp.float32))

    o_sel = jnp.moveaxis(lax.map(sel_chunk, (q_ch, idx_ch, c0)), 0, 1).reshape(B, S, N_KV, GQA_R, HEAD_DIM)

    o_win, _ = banded_attention(q, kvh(kwn), kvh(vwn), WIN - 1, 1, rel_bias)

    g = jax.nn.sigmoid((gl + b_gate).astype(jnp.float32)).reshape(B, S, N_KV, GQA_R, 3)
    o = g[..., 0:1] * o_cmp + g[..., 1:2] * o_sel + g[..., 2:3] * o_win
    return o.reshape(B, S, D_MODEL).astype(h.dtype) @ w_out

def dilated_attention(h, w_q, k_shared, v_shared, w_out, rel_bias):
    B, S, _ = h.shape
    q = (h @ w_q).reshape(B, S, N_DIL, N_KV, GQA_R, HEAD_DIM)
    outs, lses = [], []
    for gi, (window, dilation) in enumerate(DILATIONS):
        o, lse = dilated_group_attention(q[:, :, gi], k_shared[:, :, gi], v_shared[:, :, gi], dilation, window, rel_bias)
        outs.append(o)
        lses.append(lse)
    alpha = jax.nn.softmax(jnp.stack(lses, axis=-1), axis=-1)
    o = jnp.einsum('bsgrdi,bsgri->bsgrd', jnp.stack(outs, axis=-1), alpha)
    return o.reshape(B, S, D_MODEL).astype(h.dtype) @ w_out

def swiglu(h, w_up, w_down):
    a, b = jnp.split(h @ w_up, 2, axis=-1)
    return (jax.nn.silu(a) * b) @ w_down

def second_inputs(seed: int = 0) -> dict:
    key = jax.random.key(seed)
    ks = jax.random.split(key, 20)
    f32 = jnp.float32
    nrm = lambda k, shape, s: s * jax.random.normal(k, shape, f32)
    w = lambda k, shape, fan_in: jax.random.normal(k, shape, f32) * fan_in ** -0.5
    gain = lambda k, shape: 1.0 + 0.05 * jax.random.normal(k, shape, f32)
    cmp_in = CMP_BLOCK * HEAD_DIM
    return {
        "x": jax.random.normal(ks[0], (BATCH, SEQ, D_MODEL), f32),
        "rel_bias": nrm(ks[1], (NUM_BUCKETS, N_HEADS), 0.5),
        "norm_mix": gain(ks[2], (DEPTH_2, D_MODEL)),
        "norm_ffn": gain(ks[3], (DEPTH_2, D_MODEL)),
        "a_w_in": w(ks[4], (N_A_LAYERS, D_MODEL, A_IN_DIM), D_MODEL),
        "a_b_gate": nrm(ks[5], (N_A_LAYERS, 3 * N_HEADS), 0.1),
        "a_pe_k": nrm(ks[6], (N_A_LAYERS, CMP_BLOCK, HEAD_DIM), 0.1),
        "a_w1_k": w(ks[7], (N_A_LAYERS, cmp_in, CMP_HIDDEN), cmp_in),
        "a_w2_k": w(ks[8], (N_A_LAYERS, CMP_HIDDEN, HEAD_DIM), CMP_HIDDEN),
        "a_pe_v": nrm(ks[9], (N_A_LAYERS, CMP_BLOCK, HEAD_DIM), 0.1),
        "a_w1_v": w(ks[10], (N_A_LAYERS, cmp_in, CMP_HIDDEN), cmp_in),
        "a_w2_v": w(ks[11], (N_A_LAYERS, CMP_HIDDEN, HEAD_DIM), CMP_HIDDEN),
        "a_w_out": w(ks[12], (N_A_LAYERS, D_MODEL, D_MODEL), D_MODEL),
        "kv_norm": gain(ks[13], (D_MODEL,)),
        "kv_w": w(ks[14], (D_MODEL, SHARED_KV_DIM), D_MODEL),
        "b_w_q": w(ks[15], (N_B_LAYERS, D_MODEL, B_Q_DIM), D_MODEL),
        "b_w_out": w(ks[16], (N_B_LAYERS, D_MODEL, D_MODEL), D_MODEL),
        "ffn_w_up": w(ks[17], (DEPTH_2, D_MODEL, 2 * FFN_HIDDEN), D_MODEL),
        "ffn_w_down": w(ks[18], (DEPTH_2, FFN_HIDDEN, D_MODEL), FFN_HIDDEN),
        "final_norm": gain(ks[19], (D_MODEL,)),
    }

def second_block(x, rel_bias, norm_mix, norm_ffn, a_w_in, a_b_gate, a_pe_k, a_w1_k, a_w2_k, a_pe_v, a_w1_v, a_w2_v,
              a_w_out, kv_norm, kv_w, b_w_q, b_w_out, ffn_w_up, ffn_w_down, final_norm):
    B, S, _ = x.shape
    k_shared = v_shared = None
    for layer in range(DEPTH_2):
        h = rmsnorm(x, norm_mix[layer])
        if layer < N_A_LAYERS:
            i = layer
            mix = nsa_attention(h, a_w_in[i], a_b_gate[i], a_pe_k[i], a_w1_k[i], a_w2_k[i],
                                a_pe_v[i], a_w1_v[i], a_w2_v[i], a_w_out[i], rel_bias)
        else:
            if layer == N_A_LAYERS:
                kv = (rmsnorm(x, kv_norm) @ kv_w).reshape(B, S, N_DIL, 2, N_KV, HEAD_DIM)
                k_shared, v_shared = kv[:, :, :, 0], kv[:, :, :, 1]
            j = layer - N_A_LAYERS
            mix = dilated_attention(h, b_w_q[j], k_shared, v_shared, b_w_out[j], rel_bias)
        x = x + mix.astype(x.dtype)
        x = x + swiglu(rmsnorm(x, norm_ffn[layer]), ffn_w_up[layer], ffn_w_down[layer]).astype(x.dtype)
    return rmsnorm(x, final_norm)


def setup_inputs(seed=0):
    out = dict(first_inputs(seed))
    for name, value in second_inputs(seed + 1).items():
        if name != "x":
            out[name + "_2"] = value
    return out


def reference(
    x, mix_norm_g, w_in, lru_conv_w, lru_conv_b, lru_w_rg, lru_b_rg, lru_w_ig, lru_b_ig,
    lru_lambda, conf_conv_w, conf_conv_b, conf_norm_g, conf_norm_b, beta_lru, beta_conv, w_out,
    ffn_norm_g, peer_w_q, peer_sub_keys, peer_u, peer_v, final_norm_g, rel_bias_2, norm_mix_2,
    norm_ffn_2, a_w_in_2, a_b_gate_2, a_pe_k_2, a_w1_k_2, a_w2_k_2, a_pe_v_2, a_w1_v_2,
    a_w2_v_2, a_w_out_2, kv_norm_2, kv_w_2, b_w_q_2, b_w_out_2, ffn_w_up_2, ffn_w_down_2,
    final_norm_2,
):
    x = first_block(
        x, mix_norm_g, w_in, lru_conv_w, lru_conv_b, lru_w_rg, lru_b_rg, lru_w_ig, lru_b_ig,
        lru_lambda, conf_conv_w, conf_conv_b, conf_norm_g, conf_norm_b, beta_lru, beta_conv,
        w_out, ffn_norm_g, peer_w_q, peer_sub_keys, peer_u, peer_v, final_norm_g,
    )
    return second_block(
        x, rel_bias_2, norm_mix_2, norm_ffn_2, a_w_in_2, a_b_gate_2, a_pe_k_2, a_w1_k_2,
        a_w2_k_2, a_pe_v_2, a_w1_v_2, a_w2_v_2, a_w_out_2, kv_norm_2, kv_w_2, b_w_q_2,
        b_w_out_2, ffn_w_up_2, ffn_w_down_2, final_norm_2,
    )


_drawn_inputs = setup_inputs


def setup_inputs(seed=0):
    import zlib

    import numpy as np

    out = dict(_drawn_inputs(seed))
    spreads = {}
    factors = {'lru_b_rg': 6.112,
     'lru_b_ig': 5.395,
     'beta_lru': 2.999,
     'beta_conv': 2.772,
     'a_b_gate_2': 3.275,
     'a_pe_k_2': 8.0,
     'kv_norm_2': 4.103}
    for name, (base, spread) in spreads.items():
        noise = np.random.default_rng([zlib.crc32(name.encode()), seed]).standard_normal(out[name].shape)
        drawn = base * np.exp(spread * noise) if base else spread * noise
        out[name] = __import__('jax').numpy.asarray(drawn.astype(out[name].dtype))
    for name, factor in factors.items():
        out[name] = (out[name] * factor).astype(out[name].dtype)
    return out
```

```python
from contextlib import ExitStack

import numpy as np

import concourse.bass as bass
from concourse import mybir

P = 128
ALU = mybir.AluOpType
ACT = mybir.ActivationFunctionType
F32 = mybir.dt.float32
I32 = mybir.dt.int32
U32 = mybir.dt.uint32
AX_X = mybir.AxisListType.X

T = 512
TT = T // P
D = 1024
DK = D // P
DL = 512
LK = DL // P
LRU_TAPS, CONF_TAPS = 4, 31
EPS = 1e-6

PH, NKEY, TOPK = 8, 128, 16
SLOTS = PH * TOPK
HP = 2 * PH

NH, DH, NKV = 16, 64, 4
GR = NH // NKV
FK = 2816 // P
NBUCKET = 32
NCMP = (T - 32) // 16 + 1
CMP_POS = 32
NEG = -1e30
FLOOR = -1e29

ROWS = {
    "sel": (511, 639, lambda d: d >= 0),
    "win": (383, 511, lambda d: (d >= 0) & (d <= 255)),
    "dil0": (255, 383, lambda d: (d >= 0) & (d <= 128)),
    "dil1": (511, 639, lambda d: (d >= 0) & (d % 4 == 0)),
    "dil2": (511, 639, lambda d: (d >= 0) & (d % 16 == 0)),
}
CMP_LEN, CMP_COLS = 62, 55
ROW_AT = {}
_at = 0
for _name, (_top, _n, _ok) in ROWS.items():
    ROW_AT[_name] = _at
    _at += _n
ROW_AT["cmp"] = _at
ROWLEN = _at + 16 * CMP_LEN

VEC = {}
_at = 0
for _name, _n in (("mix_g", DK), ("lru_w", LRU_TAPS * LK), ("lru_b", LK), ("b_rg", 2 * LK), ("b_ig", 2 * LK),
                  ("lam", 2 * LK), ("conf_w", CONF_TAPS * LK), ("conf_b", LK), ("conf_g", LK), ("conf_nb", LK),
                  ("beta_lru", LK), ("beta_conv", LK), ("ffn_g", DK), ("fin1_g", DK), ("a_mix_g", DK),
                  ("b_mix_g", DK), ("a_ffn_g", DK), ("b_ffn_g", DK), ("kv_g", DK), ("fin2_g", DK)):
    VEC[_name] = _at
    _at += _n
NVEC = _at

RING = 4
STREAM = (("w_in", 16, DK), ("w_out", 8, DK), ("w_q", 16, DK), ("a_in", 20, DK), ("a_out", 8, DK),
          ("a_up", 44, DK), ("a_down", 16, 11), ("kv", 12, DK), ("b_q", 24, DK), ("b_out", 8, DK),
          ("b_up", 44, DK), ("b_down", 16, 11))
FIRST_UNIT, FIRST_TILE = {}, {}
_u = _o = 0
for _name, _n, _k in STREAM:
    FIRST_UNIT[_name], FIRST_TILE[_name] = _u, _o
    _u += _n
    _o += _n // 2 if _k == 11 else _n
ARENA = 32000
PAIR = 2
GROUPS = TOPK // PAIR
ROWRING = 4
NROWCHUNK = -(-ROWLEN // 512)
NCONST = 5 * P + TOPK + 1
NORMS = (("mix", DK), ("conv", LK), ("lru", LK), ("ffn", DK), ("fin1", DK), ("a_mix", DK), ("a_ffn", DK),
         ("kv", DK), ("b_mix", DK), ("b_ffn", DK), ("fin2", DK))
STATS = [x for x, _ in NORMS if x != "b_mix"]
NORM_TILES = sum(x for _, x in NORMS)


def spread(ap, n):
    return ap.unsqueeze(len(ap.shape)).broadcast_to(list(ap.shape) + [n])


class Steps:

    def __init__(self, eng, sem):
        self.eng, self.sem, self.base, self.k = eng, sem, 0, 0

    def do(self, ins):
        ins.then_inc(self.sem, 1)
        self.k += 1

    def settle(self, apart=None):
        self.eng.wait_ge(self.sem, self.base + self.k)
        if apart:
            apart(self.eng)

    def loop(self, start, end, per):
        return StepLoop(self, start, end, per)


class StepLoop:
    def __init__(self, steps, start, end, per):
        self.s, self.start, self.end, self.per = steps, start, end, per

    def __enter__(self):
        self.before = self.s.base, self.s.k
        self.fori = self.s.eng.Fori(self.start, self.end)
        i = self.fori.__enter__()
        self.s.base, self.s.k = self.before[0] + self.before[1] + (i - self.start) * self.per, 0
        return i

    def __exit__(self, *exc):
        assert exc[0] or self.s.k == self.per, (self.s.k, self.per)
        self.fori.__exit__(*exc)
        self.s.base, self.s.k = self.before[0], self.before[1] + (self.end - self.start) * self.per


def program(nc, t):
    with ExitStack() as ctx:
        def sb(name, shape, dtype=F32):
            return ctx.enter_context(nc.sbuf_tensor(name, shape, dtype))

        def sem(name):
            return ctx.enter_context(nc.semaphore(name))

        ps = ctx.enter_context(nc.psum_tensor("ps", [P, 8, 512], F32))
        h = sb("h", [P, DK, T])
        n = sb("n", [P, DK, T])
        sq = sb("sq", [P, DK, T])
        rstd = sb("rstd", [P, T])
        std = sb("std", [P, T])
        ring = sb("ring", [P, RING, 11 * P])
        vec = sb("vec", [P, NVEC])
        consts = sb("consts", [P, NCONST])
        held = sb("held", [P, 5])
        gate_bias = sb("gate_bias", [P, 3 * NH])
        tcmp = sb("tcmp", [P, NH, CMP_COLS])
        arena = sb("arena", [P, ARENA])
        rows_dram = nc.dram_tensor("bias_rows", (NH, ROWLEN), F32).ap()

        ident = consts[:, 0:P]
        ones_d = consts[:, P:2 * P]
        ones_l = consts[:, 2 * P:3 * P]
        ones_g = consts[:, 3 * P:4 * P]
        iota16 = consts[:, 4 * P:4 * P + TOPK]
        eps = consts[:, 4 * P + TOPK:4 * P + TOPK + 1]
        flip = consts[:, 4 * P + TOPK + 1:]

        class Region:

            def __init__(self, at=0):
                self.at = at

            def take(self, *shape):
                size = int(np.prod(shape))
                ap = arena[:, self.at:self.at + size]
                self.at += size
                assert self.at <= ARENA, self.at
                names = "abcd"[:len(shape)]
                if len(shape) > 1:
                    ap = ap.rearrange(f"p ({' '.join(names)}) -> p {' '.join(names)}",
                                      **dict(zip(names[:-1], shape[:-1])))
                return ap

        def col(name, k=0):
            return vec[:, VEC[name] + k:VEC[name] + k + 1]

        def bank(b):
            return ps[:, b, :]

        m = Region()
        xpad = m.take(LK, T + LRU_TAPS - 1)
        gpad = m.take(LK, T + CONF_TAPS - 1)
        sigb = m.take(LK, T)
        gelug = m.take(LK, T)
        xc = m.take(LK, T)
        cacc = m.take(LK, T)
        gw = m.take(4 * LK, P)
        rgate = m.take(2, LK, T)
        igate = m.take(2, LK, T)
        tanh_la = m.take(2, LK, T)
        wrk = m.take(2, LK, T)
        lamw = m.take(6, 2 * LK)
        onehot = tanh_la.rearrange("p a b c -> p (a b c)")[:, 0:ROWLEN]
        rowbuf = wrk.rearrange("p a b c -> p (a b c)")[:, 0:ROWLEN]
        relb = m.take(NH)
        e = Region()
        qT = e.take(HP, T)
        urow = qT.rearrange("p a b -> p (a b)").rearrange("p (s d) -> p s d", s=8)
        skT = e.take(HP, NKEY)
        s_all = e.take(TT, HP * NKEY)
        vrow_odd = e.take(4, D)
        vrow_even = n[:, :, :].rearrange("p a b -> p (a b)").rearrange("p (s d) -> p s d", s=4)
        vrow = [x[:, y:y + PAIR, :] for x in (vrow_even, vrow_odd) for y in (0, PAIR)]
        ntok = sq[:, :, :].rearrange("p a b -> p (a b)").rearrange("p (s d) -> p s d", s=TT)
        ncur = e.take(D)
        acc = e.take(2, D)
        scur, swork = e.take(2, NKEY), e.take(2, NKEY)
        cand, cwork = e.take(TOPK, TOPK), e.take(TOPK * TOPK)
        hot = e.take(2, TOPK, TOPK)
        topv, topi, topif = e.take(2, TOPK), e.take(2, TOPK).bitcast(U32), e.take(2, TOPK)
        bestv, pos = e.take(TOPK), e.take(TOPK).bitcast(U32)
        posab, posf = e.take(2, TOPK).bitcast(U32), e.take(2, TOPK)
        pick, ex, sm = e.take(2, TOPK), e.take(TOPK), e.take(4)
        expert_id = e.take(TT, SLOTS).bitcast(I32)
        gate = e.take(TT, SLOTS)
        idu, idv = e.take(ROWRING, PAIR).bitcast(I32), e.take(ROWRING, PAIR).bitcast(I32)
        dots, gel, wslot = e.take(ROWRING, PAIR), e.take(ROWRING, PAIR), e.take(ROWRING, PAIR)
        a = Region()
        proj = a.take(20, T)
        vtok = a.take(2, TT, 256)
        hg = a.take(2, 2, 2, 2 * NCMP)
        kcmp = a.take(2, NCMP)
        vcmp = a.take(256)
        gateA = a.take(TT, 3 * NH)
        w2 = a.take(2, 2, DH)
        pe2 = a.take(2, CMP_POS)
        wg = a.take(DK, 3 * NH)
        after = a.at
        w1 = a.take(2, CMP_POS, 256)
        cin = n[:, :, :].rearrange("p (a b c) t -> p a b c t", a=2, b=2)
        a2 = Region(after)
        pA, ptA = a2.take(2, 1280), a2.take(2, 1280)
        tabA = a2.take(2, 896 + CMP_COLS)
        qcurA, smA = a2.take(1, T), a2.take(2, 16)
        attn = sq
        f = Region()
        hid, silu = f.take(FK, T), f.take(2, T)
        b = Region()
        qB, kvB, vtokB = b.take(24, T), b.take(12, T), b.take(3, TT, 256)
        tabB, pB, ptB = b.take(2, 1280), b.take(2, 1280), b.take(2, 1280)
        qcurB, smB = b.take(3, T), b.take(2, 16)

        x_in, vec_in, const_in, gw_in, onehot_in, rel_in = (sem(x) for x in (
            "x_in", "vec_in", "const_in", "gw_in", "onehot_in", "rel_in"))
        w_landed = [sem(f"w_landed{j}") for j in range(RING)]
        unit_done = sem("unit_done")
        tile_drained = sem("tile_drained")
        sq_ready, ms_ready, std_ready, n_ready = sem("sq_ready"), sem("ms_ready"), sem("std_ready"), sem("n_ready")
        dve_step, act_step = sem("dve_step"), sem("act_step")
        rel_neg, row_ready, row_copied, rows_stored = sem("rel_neg"), sem("row_ready"), sem("row_copied"), sem("rows_stored")
        gw_zero, pads, gb_in = sem("gw_zero"), sem("pads"), sem("gb_in")
        sigb_ready, glu_ready, xpad_ready, gelug_ready, xc_ready = (sem(x) for x in (
            "sigb_ready", "glu_ready", "xpad_ready", "gelug_ready", "xc_ready"))
        gates_ready, gates_read, a_ready, w_ready, root_ready = (sem(x) for x in (
            "gates_ready", "gates_read", "a_ready", "w_ready", "root_ready"))
        lam_in, lam_e, lam_u, lam_ln, lam_c = (sem(x) for x in ("lam_in", "lam_e", "lam_u", "lam_ln", "lam_c"))
        ylru_ready, conv_ready, mean_ready, cen_ready, censq_ready, var_ready, cstd_ready, cn_ready, yconv_ready = (
            sem(x) for x in ("ylru_ready", "conv_ready", "mean_ready", "cen_ready", "censq_ready", "var_ready",
                             "cstd_ready", "cn_ready", "yconv_ready"))
        out_done = sem("out_done")

        def wait_tile(eng, o):
            eng.wait_ge(tile_drained, o - 3)

        def apart(dve):
            dve.tensor_copy(held[:, 0:1], held[:, 1:2])

        block = ctx.enter_context(nc.Block())

        norm_tiles = {}
        _c = 0
        for name, tiles in NORMS:
            norm_tiles[name] = _c
            _c += tiles
        squared = {name: x - (DK if name in ("b_ffn", "fin2") else 0) for name, x in norm_tiles.items()}
        norm_index = {name: i for i, name in enumerate(STATS)}

        def norm_squares(act, name, src, ready):
            for k in range(len(src)):
                ready(k)
                act.activation(sq[:, k, :], src[k], ACT.Square).then_inc(sq_ready, 1)

        def norm_root(act, name):
            act.wait_ge(ms_ready, norm_index[name] + 1)
            act.activation(std[:, :], bank(4), ACT.Sqrt, bias=eps).then_inc(std_ready, 1)

        def norm_mean(pe, name, ones):
            for k in range(dict(NORMS)[name]):
                pe.wait_ge(sq_ready, squared[name] + k + 1)
                mm = pe.matmul(bank(4), ones, sq[:, k, :], start=k == 0, stop=k == dict(NORMS)[name] - 1)
            mm.then_inc(ms_ready, 1)

        def norm_scale(dve, step, name, src, gain, dst, again=False):
            if not again:
                dve.wait_ge(std_ready, norm_index[name] + 1)
                step.do(dve.reciprocal(rstd[:, :], std[:, :]))
                step.settle()
            for k in range(len(src)):
                dve.scalar_tensor_tensor(out=dst[k], in0=src[k], scalar=col(gain, k), in1=rstd[:, :],
                                         op0=ALU.mult, op1=ALU.mult).then_inc(n_ready, 1)

        hs = [h[:, k, :] for k in range(DK)]
        ns = [n[:, k, :] for k in range(DK)]

        def stream(pe, name, rhs):
            _, units, kt = next(s for s in STREAM if s[0] == name)
            u0, o0 = FIRST_UNIT[name], FIRST_TILE[name]
            two = kt == 11

            def body(i, first=False):
                for j in range(RING):
                    o = o0 + 2 * i + j // 2 if two else o0 + RING * i + j
                    if two and j % 2 == 0:
                        pe.wait_ge(tile_drained, o - 1)
                    elif not two and not first:
                        wait_tile(pe, o)
                    pe.wait_ge(w_landed[j], 16 * (u0 // RING + 1 + i))
                    for k in range(kt):
                        mm = pe.matmul(bank(j // 2 if two else j), ring[:, j, k * P:(k + 1) * P],
                                       rhs[k + kt * (j % 2) if two else k],
                                       start=k == 0 and not (two and j % 2), stop=k == kt - 1 and not (two and not j % 2))
                    mm.then_inc(unit_done, 1)

            if u0 == 0:
                body(0, first=True)
            with pe.Fori(1 if u0 == 0 else 0, units // RING) as i:
                body(i)

        def unit_full(eng, name, i, j):
            eng.wait_ge(unit_done, FIRST_UNIT[name] + RING * i + j + 1)

        def add_residual(dve, name):
            kt = next(s for s in STREAM if s[0] == name)[2]
            per, tiles = (2, 2) if kt == 11 else (1, RING)
            with dve.Fori(0, DK // tiles) as i:
                for j in range(tiles):
                    unit_full(dve, name, i, per * j + per - 1)
                    tile = h[:, bass.ds(tiles * i + j, 1), :].rearrange("p a t -> p (a t)")
                    dve.tensor_tensor(tile, bank(j), tile, ALU.add).then_inc(tile_drained, 1)

        def residual_ready(eng, name):
            return lambda k: eng.wait_ge(tile_drained, FIRST_TILE[name] + k + 1)

        def group_std(c):
            return sq[:, LK + c, :]

        tok_turned, tok_copied, ntok_ready, sk_in, scores_full, scores_drained = (sem(x) for x in (
            "tok_turned", "tok_copied", "ntok_ready", "sk_in", "scores_full", "scores_drained"))
        ex_ready, ex_done, ids_ready, id_copied = (sem(x) for x in ("ex_ready", "ex_done", "ids_ready", "id_copied"))
        u_landed = [sem(f"u_landed{p}") for p in range(ROWRING)]
        v_landed = [sem(f"v_landed{p}") for p in range(ROWRING)]
        dots_ready, gel_ready, v_used = sem("dots_ready"), sem("gel_ready"), sem("v_used")
        acc_ready, acc_turned, peer_added = sem("acc_ready"), sem("acc_turned"), sem("peer_added")
        Q_TILES = FIRST_TILE["w_q"] + HP
        ROUNDS = PH

        def group_no(tt, i, g):
            return (tt * ROUNDS + i) * GROUPS + g

        def landings(tt, i, g):
            return 16 * PAIR * ((tt * ROUNDS + i) * (GROUPS // ROWRING) + g // ROWRING + 1)

        def peer_pe(pe):
            norm_mean(pe, "ffn", ones_d)
            pe.wait_ge(n_ready, norm_tiles["ffn"] + DK)
            for q in range(2 * TT):
                if q >= 2:
                    pe.wait_ge(tok_copied, q - 1)
                for j in range(4):
                    tr = pe.transpose(ps[:, 5 + q % 2, P * j:P * j + P], n[:, 4 * (q % 2) + j, P * (q // 2):P * (q // 2) + P],
                                      ident)
                tr.then_inc(tok_turned, 1)
            stream(pe, "w_q", ns)
            pe.wait_ge(sk_in, 16)
            pe.wait_ge(tile_drained, Q_TILES)
            for g in range(4 * TT):
                if g >= 4:
                    pe.wait_ge(scores_drained, g - 3)
                for j in range(4):
                    hp = 4 * (g % 4) + j
                    mm = pe.matmul(ps[:, g % 4, P * j:P * j + P], qT[:, hp, P * (g // 4):P * (g // 4) + P], skT[:, hp, :],
                                   start=True, stop=True)
                mm.then_inc(scores_full, 1)
            for tt in range(TT):
                pe.wait_ge(acc_ready, tt + 1)
                for q in range(2):
                    if tt:
                        pe.wait_ge(peer_added, 2 * (tt - 1) + q + 1)
                    for j in range(4):
                        tr = pe.transpose(ps[:, 5 + q, P * j:P * j + P], acc[:, 0, P * (4 * q + j):P * (4 * q + j) + P], ident)
                    tr.then_inc(acc_turned, 1)
            norm_mean(pe, "fin1", ones_d)

        def peer_act(act):
            norm_squares(act, "ffn", hs, residual_ready(act, "w_out"))
            norm_root(act, "ffn")
            with act.Fori(0, HP // RING) as i:
                for j in range(RING):
                    unit_full(act, "w_q", i, j)
                    act.copy(qT[:, bass.ds(RING * i + j, 1), :], bank(j)).then_inc(tile_drained, 1)
            for g in range(4 * TT):
                act.wait_ge(scores_full, g + 1)
                act.copy(s_all[:, g // 4, 512 * (g % 4):512 * (g % 4) + 512], bank(g % 4)).then_inc(scores_drained, 1)

            def exps(i):
                act.wait_ge(ex_ready, i + 1)
                act.activation(ex, ex, ACT.Exp).then_inc(ex_done, 1)

            def gelu(w, g):
                act.wait_ge(dots_ready, GROUPS * w + g + 1)
                act.activation(gel[:, g % ROWRING, :], dots[:, g % ROWRING, :],
                               ACT.Gelu_apprx_tanh).then_inc(gel_ready, 1)

            with act.Fori(0, ROUNDS) as i:
                exps(i)
            with act.Fori(0, (TT - 1) * ROUNDS) as w:
                gelu(w, 0)
                exps(w + ROUNDS)
                for g in range(1, GROUPS):
                    gelu(w, g)
            with act.Fori((TT - 1) * ROUNDS, TT * ROUNDS) as w:
                for g in range(GROUPS):
                    gelu(w, g)
            norm_squares(act, "fin1", hs, lambda k: act.wait_ge(peer_added, 2 * TT))
            norm_root(act, "fin1")

        def retrieve(dve, step, tt, i):
            step.do(dve.tensor_copy(scur.rearrange("p a b -> p (a b)"),
                                    s_all[:, bass.ds(tt, 1), bass.ds(2 * NKEY * i, 2 * NKEY)].rearrange("p a b -> p (a b)")))
            step.settle(apart)
            for p in range(2):
                step.do(dve.max(topv[:, p, 0:8], scur[:, p, :]))
            step.settle(apart)
            for p in range(2):
                step.do(dve.max_index(topi[:, p, 0:8], topv[:, p, 0:8], scur[:, p, :]))
                step.do(dve.match_replace(swork[:, p, :], topv[:, p, 0:8], scur[:, p, :], -3e38))
            step.settle(apart)
            for p in range(2):
                step.do(dve.max(topv[:, p, 8:16], swork[:, p, :]))
            step.settle(apart)
            for p in range(2):
                step.do(dve.max_index(topi[:, p, 8:16], topv[:, p, 8:16], swork[:, p, :]))
            yield
            step.do(dve.tensor_tensor(cand, spread(topv[:, 0, :], TOPK),
                                      topv[:, 1, :].unsqueeze(1).broadcast_to([P, TOPK, TOPK]), ALU.add))
            step.settle(apart)
            flat = cand.rearrange("p a b -> p (a b)")
            step.do(dve.max(bestv[:, 0:8], flat))
            step.do(dve.tensor_copy(topif, topi))
            step.settle(apart)
            step.do(dve.max_index(pos[:, 0:8], bestv[:, 0:8], flat))
            step.do(dve.match_replace(cwork, bestv[:, 0:8], flat, -3e38))
            step.settle(apart)
            step.do(dve.max(bestv[:, 8:16], cwork))
            step.settle(apart)
            step.do(dve.max_index(pos[:, 8:16], bestv[:, 8:16], cwork))
            yield
            dve.tensor_scalar(ex, bestv, bestv[:, 0:1], None, ALU.subtract).then_inc(ex_ready, 1)
            step.settle()
            step.do(dve.tensor_scalar(posab[:, 0, :], pos, 4, None, ALU.logical_shift_right))
            step.do(dve.tensor_scalar(posab[:, 1, :], pos, 15, None, ALU.bitwise_and))
            step.settle()
            step.do(dve.tensor_copy(posf, posab))
            step.settle()
            yield
            step.do(dve.tensor_tensor(hot, spread(posf, TOPK),
                                      iota16.unsqueeze(1).unsqueeze(1).broadcast_to([P, 2, TOPK, TOPK]), ALU.is_equal))
            step.settle()
            step.do(dve.tensor_tensor(hot, hot, topif.unsqueeze(2).broadcast_to([P, 2, TOPK, TOPK]), ALU.mult))
            step.settle()
            step.do(dve.tensor_reduce(pick, hot, AX_X, ALU.add))
            step.settle()
            dve.scalar_tensor_tensor(out=expert_id[:, bass.ds(tt, 1), bass.ds(TOPK * i, TOPK)].rearrange("p a b -> p (a b)"),
                                     in0=pick[:, 0, :], scalar=float(NKEY), in1=pick[:, 1, :],
                                     op0=ALU.mult, op1=ALU.add).then_inc(ids_ready, 1)
            yield

        RETRIEVE_STEPS = 24

        def gates(dve, step, tt, i):
            dve.wait_ge(ex_done, tt * ROUNDS + i + 1)
            step.do(dve.tensor_reduce(sm[:, 0:1], ex, AX_X, ALU.add))
            step.settle()
            step.do(dve.reciprocal(sm[:, 1:2], sm[:, 0:1]))
            step.settle()
            step.do(dve.tensor_scalar(gate[:, bass.ds(tt, 1), bass.ds(TOPK * i, TOPK)].rearrange("p a b -> p (a b)"),
                                      ex, sm[:, 1:2], None, ALU.mult))
            step.settle(apart)

        GATE_STEPS = 3

        def dot_products(dve, tt, i, g):
            p = g % ROWRING
            dve.wait_ge(u_landed[p], landings(tt, i, g))
            for r in range(PAIR):
                u = urow[:, PAIR * p + r, :]
                ins = dve.tensor_tensor_reduce(out=u, in0=u, in1=ncur, scale=1.0, scalar=0.0, op0=ALU.mult, op1=ALU.add,
                                               accum_out=dots[:, p, r:r + 1])
            ins.then_inc(dots_ready, 1)

        def weighted_sum(dve, step, tt, i, g):
            p, no = g % ROWRING, group_no(tt, i, g)
            dve.wait_ge(gel_ready, no + 1)
            step.do(dve.tensor_tensor(wslot[:, p, :], gel[:, p, :],
                                      gate[:, bass.ds(tt, 1), bass.ds(TOPK * i + PAIR * g, PAIR)].rearrange("p a b -> p (a b)"),
                                      ALU.mult))
            step.settle()
            dve.wait_ge(v_used, no + 1)
            dve.wait_ge(v_landed[p], landings(tt, i, g))
            for r in range(PAIR):
                ins = dve.scalar_tensor_tensor(out=acc[:, r, :], in0=vrow[p][:, r, :], scalar=wslot[:, p, r:r + 1],
                                               in1=acc[:, r, :], op0=ALU.mult, op1=ALU.add)
            ins.then_inc(v_used, 1)

        SUM_STEPS = 1

        def peer_dve(dve, step):
            norm_scale(dve, step, "ffn", hs, "ffn_g", ns)
            for q in range(2 * TT):
                dve.wait_ge(tok_turned, q + 1)
                dve.tensor_copy(ntok[:, q // 2, 512 * (q % 2):512 * (q % 2) + 512], bank(5 + q % 2)).then_inc(tok_copied, 1)
            dve.wait_ge(scores_drained, 4 * TT)
            dve.memset(sm, 0.0).then_inc(v_used, 1)
            with step.loop(0, ROUNDS, RETRIEVE_STEPS + GATE_STEPS) as i:
                for _ in retrieve(dve, step, 0, i):
                    pass
                gates(dve, step, 0, i)

            def tile(tt, last):
                step.do(dve.tensor_copy(ncur, ntok[:, bass.ds(tt, 1), :].rearrange("p a b -> p (a b)")))
                step.do(dve.memset(acc, 0.0))
                step.settle(apart)
                per = GROUPS * SUM_STEPS + (0 if last else RETRIEVE_STEPS + GATE_STEPS)
                with step.loop(0, ROUNDS, per) as i:
                    parts = [] if last else retrieve(dve, step, tt + 1, i)
                    for g in range(GROUPS):
                        dot_products(dve, tt, i, g)
                        if g >= 2:
                            weighted_sum(dve, step, tt, i, g - 2)
                        if g < 4 and not last:
                            next(parts)
                        if g == 6 and not last:
                            gates(dve, step, tt + 1, i)
                    weighted_sum(dve, step, tt, i, GROUPS - 2)
                    weighted_sum(dve, step, tt, i, GROUPS - 1)
                dve.wait_ge(v_used, group_no(tt, ROUNDS - 1, GROUPS - 1) + 2)
                step.settle()
                dve.tensor_tensor(acc[:, 0, :], acc[:, 0, :], acc[:, 1, :], ALU.add).then_inc(acc_ready, 1)
                for q in range(2):
                    dve.wait_ge(acc_turned, 2 * tt + q + 1)
                    part = h[:, 4 * q:4 * q + 4, bass.ds(P * tt, P)]
                    dve.tensor_tensor(part, ps[:, 5 + q, :].rearrange("p (a b) -> p a b", a=4), part,
                                      ALU.add).then_inc(peer_added, 1)
                return 2 + ROUNDS * per

            with step.loop(0, TT - 1, 2 + ROUNDS * (GROUPS * SUM_STEPS + RETRIEVE_STEPS + GATE_STEPS)) as tt:
                tile(tt, False)
            tile(TT - 1, True)
            norm_scale(dve, step, "fin1", hs, "fin1_g", hs)

        def peer_pool(pool):
            pool.wait_ge(n_ready, norm_tiles["lru"] + LK)
            pool.dma_start(skT, t["sub_keys"]).then_inc(sk_in, 16)

            def gather(tt, i, g, table, ids, rows, landed, used, least, copies):
                p = g % ROWRING
                if least is not None:
                    pool.wait_ge(used, least)
                    pool.tensor_tensor(held[:, 4:5], held[:, 1:2], held[:, 1:2], ALU.add)
                pool.tensor_copy(ids[:, p, :], expert_id[:, bass.ds(tt, 1), bass.ds(TOPK * i + PAIR * g, PAIR)]
                                 .rearrange("p a b -> p (a b)")).then_inc(id_copied, 1)
                pool.wait_ge(id_copied, copies)
                pool.tensor_tensor(held[:, 3:4], held[:, 1:2], held[:, 1:2], ALU.add)
                for r in range(PAIR):
                    pool.indirect_dma_start(rows[:, r, :], None, t[table],
                                            bass.IndirectOffsetOnAxis(ap=ids[:, p, r:r + 1], axis=0)
                                            ).then_inc(landed[p], 16)

            def round_(tt, i, first=False):
                for g in range(GROUPS):
                    p, no = g % ROWRING, group_no(tt, i, g)
                    fresh = first and g < ROWRING
                    gather(tt, i, g, "peer_u", idu, urow[:, PAIR * p:PAIR * p + PAIR, :], u_landed, dots_ready,
                           None if fresh else no - ROWRING + 1, 2 * no + 1)
                    gather(tt, i, g, "peer_v", idv, vrow[p], v_landed, v_used,
                           None if fresh else no - ROWRING + 2, 2 * no + 2)

            pool.wait_ge(ids_ready, ROUNDS)
            round_(0, 0, True)
            with pool.Fori(1, ROUNDS) as i:
                round_(0, i)
            with pool.Fori(1, TT) as tt:
                with pool.Fori(0, ROUNDS) as i:
                    pool.wait_ge(ids_ready, ROUNDS * tt + ROUNDS)
                    round_(tt, i)

        silu_ready = {x: sem(f"silu_ready_{x}") for x in "ab"}

        def swiglu_pe(pe, l):
            norm_mean(pe, f"{l}_ffn", ones_d)
            pe.wait_ge(n_ready, norm_tiles[f"{l}_ffn"] + DK)
            stream(pe, f"{l}_up", ns)
            pe.wait_ge(tile_drained, FIRST_TILE[f"{l}_up"] + 2 * FK)
            stream(pe, f"{l}_down", [hid[:, k, :] for k in range(FK)])

        def swiglu_act(act, l):
            act.wait_ge(unit_done, FIRST_UNIT[f"{l}_out"] + DK)
            norm_squares(act, f"{l}_ffn", hs, residual_ready(act, f"{l}_out"))
            norm_root(act, f"{l}_ffn")
            o0 = FIRST_TILE[f"{l}_up"]
            with act.Fori(0, FK // 2) as i:
                for pr in range(2):
                    unit_full(act, f"{l}_up", i, 2 * pr)
                    act.wait_ge(tile_drained, o0 + 4 * i + 2 * pr - 2)
                    act.activation(silu[:, pr, :], bank(2 * pr), ACT.Silu).then_inc(silu_ready[l], 1)

        def swiglu_dve(dve, step, l):
            norm_scale(dve, step, f"{l}_ffn", hs, f"{l}_ffn_g", ns)
            with dve.Fori(0, FK // 2) as i:
                for pr in range(2):
                    dve.wait_ge(silu_ready[l], 2 * i + pr + 1)
                    unit_full(dve, f"{l}_up", i, 2 * pr + 1)
                    dve.tensor_tensor(hid[:, bass.ds(2 * i + pr, 1), :].rearrange("p a t -> p (a t)"), silu[:, pr, :],
                                      bank(2 * pr + 1), ALU.mult).then_inc(tile_drained, 2)
            add_residual(dve, f"{l}_down")

        class Layer:
            pass

        LA, LB = Layer(), Layer()
        LA.p, LA.pt, LA.tab, LA.q, LA.sm, LA.banks = pA, ptA, tabA, qcurA, smA, 2
        LB.p, LB.pt, LB.tab, LB.q, LB.sm, LB.banks = pB, ptB, tabB, qcurB, smB, 3
        LA.name, LB.name = "a", "b"
        for L in (LA, LB):
            (L.scores_ready, L.bank_read, L.max_ready, L.exp_done, L.probs_ready, L.turned, L.pt_copied, L.pv_done,
             L.q_staged, L.o_drained) = (sem(f"{x}_{L.name}") for x in (
                 "scores_ready", "bank_read", "max_ready", "exp_done", "probs_ready", "turned", "pt_copied", "pv_done",
                 "q_staged", "o_drained"))
            L.tab_in = [sem(f"tab_in_{L.name}{x}") for x in range(2)]
            L.tab_dmas = 3

        def branches(L, gp, half, qt):
            g, lo = 2 * gp + half, 64 * half
            rows = slice(lo, lo + 64)
            keys = P * (qt + 1)
            if L is LA:
                k0 = max(0, qt - 2)
                wide = P * (qt + 1 - k0)
                return [
                    (0, 0, keys, 0, proj[rows, 12 + gp, 0:keys], L.tab[:, half, 512 - keys:512],
                     [vtok[:, 0, x, 64 * g:64 * g + 64] for x in range(qt + 1)]),
                    (1, 0, wide, 0, proj[rows, 16 + gp, P * k0:keys], L.tab[:, half, 896 - wide:896],
                     [vtok[:, 1, x, 64 * g:64 * g + 64] for x in range(k0, qt + 1)]),
                    (1, 384, NCMP, 0, kcmp[rows, gp, :], L.tab[:, half, 896 + 24 - 8 * qt:896 + 24 - 8 * qt + NCMP],
                     [vcmp[0:NCMP, 64 * g:64 * g + 64]]),
                ]
            k0 = max(0, qt - 1)
            wide = P * (qt + 1 - k0)
            out = [(0, 0, wide, 0, kvB[rows, gp, P * k0:keys], L.tab[:, half, 256 - wide:256],
                    [vtokB[:, 0, x, 64 * g:64 * g + 64] for x in range(k0, qt + 1)])]
            for d in (1, 2):
                out.append((d, 0, keys, d, kvB[rows, 2 * d + gp, 0:keys],
                            L.tab[:, half, 256 + 512 * d - keys:256 + 512 * d],
                            [vtokB[:, d, x, 64 * g:64 * g + 64] for x in range(qt + 1)]))
            return out

        def blocks(L, gp, half, qt):
            out, at = [], 0
            for _, _, width, _, _, _, values in branches(L, gp, half, qt):
                for x, v in enumerate(values):
                    out.append((at + P * x, min(P, width - P * x), v))
                at += width
            return out

        def chunks(L, qt):
            return -(-len(blocks(L, 0, 0, qt)) // 4)

        def chunk_no(L, s):
            return sum(chunks(L, x % TT) for x in range(s))

        STEPS = 2 * TT

        def attn_pe(pe, L):
            per_pair = chunk_no(L, STEPS)
            for gp in range(2):
                with pe.Fori(4 * gp, 4 * gp + 4) as it:
                    def scores(s):
                        half, qt = divmod(s, TT)
                        use = L.banks * s
                        seen = -1
                        for bk, c, width, q, keys, _, _ in branches(L, gp, half, qt):
                            if bk != seen and use + bk >= 4:
                                pe.wait_ge(L.bank_read, it * (STEPS * L.banks) + use + bk - 3)
                            mm = pe.matmul(ps[:, (use + bk) % 4, c:c + width],
                                           L.q[64 * half:64 * half + 64, q, P * qt:P * qt + P], keys, start=True, stop=True)
                            mm.then_inc(L.scores_ready, 1)
                            seen = bk

                    def turn(s):
                        half, qt = divmod(s, TT)
                        pe.wait_ge(L.probs_ready, it * STEPS + s + 1)
                        bl = blocks(L, gp, half, qt)
                        for c in range(chunks(L, qt)):
                            no = chunk_no(L, s) + c
                            if no >= 2:
                                pe.wait_ge(L.pt_copied, it * per_pair + no - 1)
                            for x, (at, width, _) in enumerate(bl[4 * c:4 * c + 4]):
                                tr = pe.transpose(ps[0:width, 4 + no % 2, P * x:P * x + P], L.p[:, s % 2, at:at + width], ident)
                            tr.then_inc(L.turned, 1)

                    def values(s):
                        half, qt = divmod(s, TT)
                        pe.wait_ge(L.pt_copied, it * per_pair + chunk_no(L, s + 1))
                        bl = blocks(L, gp, half, qt)
                        for x, (_, width, v) in enumerate(bl):
                            mm = pe.matmul(ps[64 * half:64 * half + 64, 6, P * qt:P * qt + P], v,
                                           L.pt[0:width, s % 2, P * x:P * x + P], start=x == 0, stop=x == len(bl) - 1)
                        mm.then_inc(L.pv_done, 1)

                    pe.wait_ge(L.q_staged, it + 1)
                    pe.wait_ge(L.o_drained, it + 1)
                    scores(0)
                    for s in range(STEPS):
                        if s + 1 < STEPS:
                            scores(s + 1)
                        if s:
                            values(s - 1)
                        turn(s)
                    values(STEPS - 1)

        def attn_dve(dve, step, L):
            nb = len(branches(L, 0, 0, 0))
            A = L is LA
            per = STEPS * (7 if A else 3)
            for gp in range(2):
                with step.loop(4 * gp, 4 * gp + 4, per) as it:
                    def row_max(s):
                        half, qt = divmod(s, TT)
                        mx = L.sm[:, s % 2, 0:3]
                        if qt == 0:
                            dve.wait_ge(L.tab_in[half], (it + 1) * (16 * L.tab_dmas))
                        if s >= 2:
                            dve.wait_ge(L.turned, it * chunk_no(L, STEPS) + chunk_no(L, s - 1))
                        dve.wait_ge(L.scores_ready, it * (STEPS * nb) + nb * (s + 1))
                        apart(dve)
                        at = 0
                        for x, (bk, c, width, _, _, tab, _) in enumerate(branches(L, gp, half, qt)):
                            ins = dve.tensor_tensor_reduce(
                                out=L.p[:, s % 2, at:at + width], in0=ps[:, (L.banks * s + bk) % 4, c:c + width], in1=tab,
                                scale=1.0, scalar=FLOOR, op0=ALU.add, op1=ALU.max, accum_out=mx[:, x:x + 1])
                            at += width
                            if A and x == 1:
                                step.do(ins)
                            else:
                                ins.then_inc(L.bank_read, 1)
                        dve.wait_ge(L.bank_read, it * (STEPS * L.banks) + L.banks * (s + 1))
                        if A:
                            dve.tensor_scalar(L.sm[:, s % 2, 3:6], mx, -1.0, None, ALU.mult).then_inc(L.max_ready, 1)
                            return
                        step.do(dve.tensor_reduce(L.sm[:, s % 2, 12:13], mx, AX_X, ALU.max))
                        step.settle()
                        dve.tensor_scalar(L.sm[:, s % 2, 3:4], L.sm[:, s % 2, 12:13], -1.0, None,
                                          ALU.mult).then_inc(L.max_ready, 1)

                    def normalise(s):
                        half, qt = divmod(s, TT)
                        dve.wait_ge(L.exp_done, it * STEPS + s + 1)
                        den, inv = L.sm[:, s % 2, 6:9], L.sm[:, s % 2, 9:12]
                        if A:
                            step.do(dve.tensor_scalar(inv, den, 1e-30, None, ALU.max))
                            step.settle()
                            step.do(dve.reciprocal(inv, inv))
                            step.settle()
                            g3 = gateA[:, qt, bass.ds(3 * (it - 4 * gp) + 3 * GR * (2 * gp + half), 3)]
                            step.do(dve.tensor_tensor(inv[:, 2:3], inv[:, 2:3], g3[:, 0:1], ALU.mult))
                            step.do(dve.tensor_tensor(inv[:, 0:2], inv[:, 0:2], g3[:, 1:3], ALU.mult))
                            step.settle()
                        else:
                            step.do(dve.tensor_reduce(L.sm[:, s % 2, 13:14], den, AX_X, ALU.add))
                            step.settle()
                            step.do(dve.reciprocal(inv[:, 0:1], L.sm[:, s % 2, 13:14]))
                            step.settle()
                        at = 0
                        br = branches(L, gp, half, qt)
                        if not A:
                            br = [(0, 0, sum(x[2] for x in br))]
                        for x, b_ in enumerate(br):
                            pr = L.p[:, s % 2, at:at + b_[2]]
                            ins = dve.tensor_scalar(pr, pr, inv[:, x:x + 1], None, ALU.mult)
                            if x < len(br) - 1:
                                step.do(ins)
                            at += b_[2]
                        ins.then_inc(L.probs_ready, 1)

                    dve.wait_ge(L.o_drained, it + 1)
                    row_max(0)
                    for s in range(STEPS):
                        if s + 1 < STEPS:
                            row_max(s + 1)
                        normalise(s)

        def attn_act(act, L):
            A = L is LA
            per_pair = chunk_no(L, STEPS)
            act.copy(held[:, 2:3], held[:, 1:2]).then_inc(L.o_drained, 1)
            for gp in range(2):
                with act.Fori(4 * gp, 4 * gp + 4) as it:
                    def exponentials(s):
                        half, qt = divmod(s, TT)
                        act.wait_ge(L.max_ready, it * STEPS + s + 1)
                        at = 0
                        for x, b_ in enumerate(branches(L, gp, half, qt)):
                            pr = L.p[:, s % 2, at:at + b_[2]]
                            y = 3 + x if A else 3
                            ins = act.activation(pr, pr, ACT.Exp, bias=L.sm[:, s % 2, y:y + 1],
                                                 accum_out=L.sm[:, s % 2, 6 + x:7 + x])
                            at += b_[2]
                        ins.then_inc(L.exp_done, 1)

                    def copy_turned(s):
                        half, qt = divmod(s, TT)
                        if s >= 2:
                            act.wait_ge(L.pv_done, it * STEPS + s - 1)
                        bl = blocks(L, gp, half, qt)
                        for c in range(chunks(L, qt)):
                            no = chunk_no(L, s) + c
                            act.wait_ge(L.turned, it * per_pair + no + 1)
                            part = bl[4 * c:4 * c + 4]
                            full = sum(w == P for _, w, _ in part)
                            src, dst = bank(4 + no % 2), L.pt[:, s % 2, 512 * c:min(512 * c + 512, 1280)]
                            if full:
                                ins = act.copy(dst[:, 0:P * full], src[:, 0:P * full])
                            if full < len(part):
                                w = part[-1][1]
                                ins = act.copy(dst[0:w, P * full:P * full + P], src[0:w, P * full:P * full + P])
                            ins.then_inc(L.pt_copied, 1)

                    exponentials(0)
                    for s in range(STEPS):
                        if s + 1 < STEPS:
                            exponentials(s + 1)
                        copy_turned(s)
                    act.wait_ge(L.pv_done, it * STEPS + STEPS)
                    act.copy(attn[:, bass.ds(it, 1), :].rearrange("p o (a t) -> p (o a) t", a=TT),
                             bank(6).rearrange("p (a t) -> p a t", a=TT)[:, :, ::-1]).then_inc(L.o_drained, 1)

        def attn_pool(pool, L, src, tiles):
            with pool.Fori(0, 8) as it:
                pool.wait_ge(L.o_drained, it + 1)
                for d in range(tiles):
                    ins = pool.tensor_copy(L.q[:, d, :].rearrange("p (a t) -> p a t", a=TT)[:, :, ::-1],
                                           src[:, bass.ds(8 * d + it, 1), :].rearrange("p o (a t) -> p (o a) t", a=TT))
                ins.then_inc(L.q_staged, 1)

        def attn_tables(sp, L):
            def toeplitz(head, name, width):
                return bass.AP(tensor=rows_dram.tensor, offset=head * ROWLEN + ROW_AT[name], ap=[[1, P], [1, width]])

            for it in range(8):
                gp, r = divmod(it, GR)
                for half in range(2):
                    head = (2 * gp + half) * GR + r
                    if it:
                        sp.wait_ge(L.bank_read, ((it - 1) * STEPS + TT * (half + 1)) * L.banks)
                    if L is LA:
                        parts = [(0, 512, toeplitz(head, "sel", 512)), (512, 896, toeplitz(head, "win", 384)),
                                 (896, 896 + CMP_COLS, tcmp[:, head, :])]
                    else:
                        parts = [(0, 256, toeplitz(head, "dil0", 256)), (256, 768, toeplitz(head, "dil1", 512)),
                                 (768, 1280, toeplitz(head, "dil2", 512))]
                    for c0, c1, src in parts:
                        sp.dma_start(L.tab[:, half, c0:c1], src).then_inc(L.tab_in[half], 16)

        wg_in, w1_in, w2_in, pe_in, tcmp_in = (sem(x) for x in ("wg_in", "w1_in", "w2_in", "pe_in", "tcmp_in"))
        gl_ready, gl_biased, gate_ready, vt_turned, vt_copied, cin_ready, hc_ready, hg_ready, cmp_ready, cmp_copied = (
            sem(x) for x in ("gl_ready", "gl_biased", "gate_ready", "vt_turned", "vt_copied", "cin_ready", "hc_ready",
                             "hg_ready", "cmp_ready", "cmp_copied"))
        vt_turned_b, vt_copied_b, gate_flipped = sem("vt_turned_b"), sem("vt_copied_b"), sem("gate_flipped")

        def turn_values(pe, src, first, groups, turned, copied):
            for q in range(2 * groups):
                x, tp = divmod(q, 2)
                if q >= 2:
                    pe.wait_ge(copied, q - 1)
                for j in range(4):
                    tt, gp = 2 * tp + j // 2, j % 2
                    tr = pe.transpose(ps[:, 6 + q % 2, P * j:P * j + P], src[:, first[x] + gp, P * tt:P * tt + P], ident)
                tr.then_inc(turned, 1)

        def copy_values(dve, dst, groups, turned, copied):
            for q in range(2 * groups):
                x, tp = divmod(q, 2)
                dve.wait_ge(turned, q + 1)
                dve.tensor_copy(dst[:, x, 2 * tp:2 * tp + 2, :], bank(6 + q % 2)).then_inc(copied, 1)

        def layer_a_pe(pe):
            norm_mean(pe, "a_mix", ones_d)
            pe.wait_ge(n_ready, norm_tiles["a_mix"] + DK)
            stream(pe, "a_in", ns)
            pe.wait_ge(wg_in, 16)
            for tt in range(TT):
                for k in range(DK):
                    mm = pe.matmul(ps[:, 5, 48 * tt:48 * tt + 48], n[:, k, P * tt:P * tt + P], wg[:, k, :],
                                   start=k == 0, stop=k == DK - 1)
            mm.then_inc(gl_ready, 1)
            pe.wait_ge(tile_drained, FIRST_TILE["a_in"] + 20)
            turn_values(pe, proj, (14, 18), 2, vt_turned, vt_copied)
            pe.wait_ge(w1_in, 64)
            for kv in range(2):
                pe.wait_ge(cin_ready, 2 * kv + 2)
                for half in range(2):
                    for tile in range(2):
                        for p in range(CMP_POS):
                            rows = slice(64 * half, 64 * half + 64)
                            mm = pe.matmul(ps[:, 2 * kv + half, 62 * tile:62 * tile + 62], w1[rows, kv, p, P * tile:P * tile + P],
                                           cin[rows, kv, p // 16, :, p:p + 16 * (NCMP - 1) + 1:16],
                                           start=p == 0, stop=p == CMP_POS - 1)
                    mm.then_inc(hc_ready, 1)
            pe.wait_ge(w2_in, 16)
            pe.wait_ge(hg_ready, 4)
            for half in range(2):
                for tile in range(2):
                    pe.matmul(ps[64 * half:64 * half + 64, 4, 0:62], w2[:, 0, tile, :], hg[:, 0, tile, half, :],
                              start=tile == 0, stop=tile == 1)
            for g in range(NKV):
                u, half = divmod(g, 2)
                for tile in range(2):
                    mm = pe.matmul(ps[0:NCMP, 5, 64 * g:64 * g + 64], hg[:, 1, tile, half, NCMP * u:NCMP * u + NCMP],
                                   w2[:, 1, tile, :], start=tile == 0, stop=tile == 1)
            mm.then_inc(cmp_ready, 1)
            pe.wait_ge(gate_ready, 1)
            pe.wait_ge(vt_copied, 4)
            pe.matmul(ps[:, 7, 0:TT * 48], flip, gateA.rearrange("p a b -> p (a b)"), start=True,
                      stop=True).then_inc(gate_flipped, 1)
            pe.wait_ge(cmp_copied, 2)
            attn_pe(pe, LA)
            pe.wait_ge(LA.o_drained, 9)
            stream(pe, "a_out", [attn[:, k, :] for k in range(DK)])

        def layer_a_act(act):
            norm_squares(act, "a_mix", hs, lambda k: act.wait_ge(n_ready, norm_tiles["fin1"] + k + 1))
            act.wait_ge(n_ready, norm_tiles["fin1"] + DK)
            norm_root(act, "a_mix")
            with act.Fori(0, 2) as i:
                for j in range(RING):
                    unit_full(act, "a_in", i, j)
                    act.mul(proj[:, bass.ds(RING * i + j, 1), :], bank(j), DH ** -0.5).then_inc(tile_drained, 1)
            with act.Fori(2, 5) as i:
                for j in range(RING):
                    unit_full(act, "a_in", i, j)
                    act.copy(proj[:, bass.ds(RING * i + j, 1), :], bank(j)).then_inc(tile_drained, 1)
            act.wait_ge(gl_biased, 1)
            act.activation(gateA, gateA, ACT.Sigmoid).then_inc(gate_ready, 1)
            for kv in range(2):
                for half in range(2):
                    act.wait_ge(hc_ready, 2 * kv + half + 1)
                    act.activation(hg[:, kv, :, half, :], ps[:, 2 * kv + half, 0:124].rearrange("p (a b) -> p a b", a=2),
                                   ACT.Gelu_apprx_tanh).then_inc(hg_ready, 1)
            act.wait_ge(cmp_ready, 1)
            act.copy(kcmp, ps[:, 4, 0:62]).then_inc(cmp_copied, 1)
            act.copy(vcmp[0:NCMP, :], ps[0:NCMP, 5, 0:256]).then_inc(cmp_copied, 1)
            attn_act(act, LA)

        def layer_a_dve(dve, step):
            norm_scale(dve, step, "a_mix", hs, "a_mix_g", ns)
            dve.wait_ge(gl_ready, 1)
            dve.wait_ge(gb_in, 16)
            dve.tensor_tensor(gateA, ps[:, 5, 0:TT * 48].rearrange("p (a b) -> p a b", a=TT),
                              gate_bias[:, :].unsqueeze(1).broadcast_to([P, TT, 48]), ALU.add).then_inc(gl_biased, 1)
            dve.wait_ge(pe_in, 16)
            dve.wait_ge(tile_drained, FIRST_TILE["a_in"] + 12)
            for kv in range(2):
                for ab in range(2):
                    for u in range(2):
                        ins = dve.tensor_tensor(cin[:, kv, ab, u, :].rearrange("p (b c) -> p b c", c=16),
                                                proj[:, 8 + 2 * kv + u, :].rearrange("p (b c) -> p b c", c=16),
                                                pe2[:, kv, 16 * ab:16 * ab + 16].unsqueeze(1).broadcast_to([P, T // 16, 16]),
                                                ALU.add)
                    ins.then_inc(cin_ready, 1)
            copy_values(dve, vtok, 2, vt_turned, vt_copied)
            dve.wait_ge(gate_flipped, 1)
            step.do(dve.tensor_copy(gateA.rearrange("p a b -> p (a b)"), ps[:, 7, 0:TT * 48]))
            step.settle()
            attn_dve(dve, step, LA)
            add_residual(dve, "a_out")

        def layer_a_pool(pool):
            pool.wait_ge(rows_stored, 16)
            for x in range(8):
                src = bass.AP(tensor=rows_dram.tensor, offset=ROW_AT["cmp"] + x,
                              ap=[[CMP_LEN, 16], [ROWLEN, NH], [1, CMP_COLS]])
                pool.dma_start(tcmp[16 * x:16 * x + 16, :, :], src).then_inc(tcmp_in, 16)
            pool.wait_ge(peer_added, 2 * TT)
            pool.dma_start(wg, t["a_gate"]).then_inc(wg_in, 16)
            pool.dma_start(pe2, t["pe"]).then_inc(pe_in, 16)
            pool.dma_start(w2, t["w2"]).then_inc(w2_in, 16)
            for half in range(2):
                for kv in range(2):
                    pool.dma_start(w1[64 * half:64 * half + 64, kv], t["w1"][:, kv]).then_inc(w1_in, 16)
            pool.wait_ge(tile_drained, FIRST_TILE["a_in"] + 8)
            pool.wait_ge(hc_ready, 4)
            attn_pool(pool, LA, proj, 1)

        def layer_a_sp(sp):
            sp.wait_ge(tcmp_in, 128)
            sp.wait_ge(hc_ready, 4)
            attn_tables(sp, LA)

        def layer_b_pe(pe):
            norm_mean(pe, "kv", ones_d)
            pe.wait_ge(n_ready, norm_tiles["kv"] + DK)
            stream(pe, "kv", ns)
            pe.wait_ge(tile_drained, FIRST_TILE["kv"] + 12)
            turn_values(pe, kvB, (6, 8, 10), 3, vt_turned_b, vt_copied_b)
            pe.wait_ge(n_ready, norm_tiles["b_mix"] + DK)
            stream(pe, "b_q", ns)
            pe.wait_ge(tile_drained, FIRST_TILE["b_q"] + 24)
            pe.wait_ge(vt_copied_b, 6)
            attn_pe(pe, LB)
            pe.wait_ge(LB.o_drained, 9)
            stream(pe, "b_out", [attn[:, k, :] for k in range(DK)])

        def layer_b_act(act):
            norm_squares(act, "kv", hs, residual_ready(act, "a_down"))
            norm_root(act, "kv")
            with act.Fori(0, 3) as i:
                for j in range(RING):
                    unit_full(act, "kv", i, j)
                    act.copy(kvB[:, bass.ds(RING * i + j, 1), :], bank(j)).then_inc(tile_drained, 1)
            with act.Fori(0, 6) as i:
                for j in range(RING):
                    unit_full(act, "b_q", i, j)
                    act.mul(qB[:, bass.ds(RING * i + j, 1), :], bank(j), DH ** -0.5).then_inc(tile_drained, 1)
            attn_act(act, LB)

        def layer_b_dve(dve, step):
            norm_scale(dve, step, "kv", hs, "kv_g", ns)
            dve.wait_ge(unit_done, FIRST_UNIT["kv"] + 12)
            norm_scale(dve, step, "b_mix", hs, "b_mix_g", ns, again=True)
            copy_values(dve, vtokB, 3, vt_turned_b, vt_copied_b)
            attn_dve(dve, step, LB)
            add_residual(dve, "b_out")

        def layer_b_pool(pool):
            pool.wait_ge(tile_drained, FIRST_TILE["b_q"] + 24)
            attn_pool(pool, LB, qB, 3)

        def layer_b_sp(sp):
            sp.wait_ge(tile_drained, FIRST_TILE["b_down"] - 2 * FK - DK)
            attn_tables(sp, LB)

        @block.sync
        def _(sp):
            for k in range(2):
                sp.dma_start(h[:, 4 * k:4 * k + 4, :], t["x"][:, 4 * k:4 * k + 4, :]).then_inc(x_in, 16)
            sp.dma_start(consts[:, :], t["consts"]).then_inc(const_in, 16)
            sp.dma_start(vec[:, :], t["vec"]).then_inc(vec_in, 16)
            for name, units, kt in STREAM:
                u0 = FIRST_UNIT[name]
                if name == "a_out":
                    layer_a_sp(sp)
                if name == "b_out":
                    layer_b_sp(sp)

                def load(i, j, first):
                    if not first:
                        sp.wait_ge(unit_done, u0 + RING * i + j - RING + 1)
                    sp.dma_start(ring[:, j, 0:kt * P], 
                                 t[name][bass.ds(RING * i + j, 1)].rearrange("u p c -> p (u c)")).then_inc(w_landed[j], 16)

                if u0 == 0:
                    for j in range(RING):
                        load(0, j, True)
                with sp.Fori(1 if u0 == 0 else 0, units // RING) as i:
                    for j in range(RING):
                        load(i, j, False)
            sp.wait_ge(n_ready, NORM_TILES)
            sp.dma_start(t["out"], n[:, :, :]).then_inc(out_done, 16)
            sp.wait_ge(out_done, 16)

        @block.tensor
        def _(pe):
            pe.wait_ge(onehot_in, 16)
            pe.wait_ge(rel_in, 16)
            pe.wait_ge(rel_neg, 1)
            for c in range(NROWCHUNK):
                if c >= 2:
                    pe.wait_ge(row_copied, c - 1)
                w = min(512, ROWLEN - 512 * c)
                pe.matmul(ps[0:NH, 5 + c % 2, 0:w], relb[0:NBUCKET + 1, :], onehot[0:NBUCKET + 1, 512 * c:512 * c + w],
                          start=True, stop=True).then_inc(row_ready, 1)
            pe.wait_ge(const_in, 16)
            norm_mean(pe, "mix", ones_d)
            pe.wait_ge(n_ready, norm_tiles["mix"] + DK)
            stream(pe, "w_in", ns)
            pe.wait_ge(gw_in, 32)
            for c in range(LK):
                pe.wait_ge(xc_ready, c + 1)
                pe.wait_ge(row_copied, NROWCHUNK)
                for g in range(4):
                    if c >= 1:
                        pe.wait_ge(gates_read, 4 * (c - 1) + g + 1)
                    pe.matmul(bank(4 + g), gw[:, 4 * g + c, :], xc[:, c, :], start=True,
                              stop=True).then_inc(gates_ready, 1)
            for c in range(LK):
                pe.wait_ge(conv_ready, c + 1)
                if c == 0:
                    pe.wait_ge(gates_read, 4 * LK)
                pe.matmul(bank(4 + c), ones_g, cacc[:, c, :], start=True, stop=True).then_inc(mean_ready, 1)
            for c in range(LK):
                pe.wait_ge(cen_ready, c + 1)
                pe.wait_ge(censq_ready, c + 1)
                pe.matmul(bank(4 + c), ones_g, sq[:, c, :], start=True, stop=True).then_inc(var_ready, 1)
            pe.wait_ge(cstd_ready, LK)
            norm_mean(pe, "conv", ones_l)
            norm_mean(pe, "lru", ones_l)
            pe.wait_ge(n_ready, norm_tiles["lru"] + LK)
            stream(pe, "w_out", ns)
            peer_pe(pe)
            layer_a_pe(pe)
            swiglu_pe(pe, "a")
            layer_b_pe(pe)
            swiglu_pe(pe, "b")
            norm_mean(pe, "fin2", ones_d)

        @block.scalar
        def _(act):
            act.dma_start(onehot[0:NBUCKET + 1, :], t["onehot"]).then_inc(onehot_in, 16)
            act.dma_start(relb[0:NBUCKET, :], t["rel_bias_2"]).then_inc(rel_in, 16)
            act.wait_ge(const_in, 16)
            norm_squares(act, "mix", hs, lambda k: act.wait_ge(x_in, 32) if k == 0 else None)
            for c in range(NROWCHUNK):
                act.wait_ge(row_ready, c + 1)
                w = min(512, ROWLEN - 512 * c)
                act.copy(rowbuf[0:NH, 512 * c:512 * c + w], ps[0:NH, 5 + c % 2, 0:w]).then_inc(row_copied, 1)
            norm_root(act, "mix")
            act.wait_ge(row_copied, NROWCHUNK)
            act.dma_start(rows_dram, rowbuf[0:NH, :]).then_inc(rows_stored, 16)
            act.wait_ge(lam_in, 1)
            act.activation(lamw[:, 1, :], lamw[:, 0, :], ACT.Exp, scale=-1.0).then_inc(lam_e, 1)
            act.wait_ge(lam_u, 1)
            act.activation(lamw[:, 3, :], lamw[:, 2, :], ACT.Ln).then_inc(lam_ln, 1)
            for c in range(LK):
                act.wait_ge(unit_done, 2 * c + 2)
                act.activation(sigb[:, c, :], bank((2 * c + 1) % 4), ACT.Sigmoid).then_inc(sigb_ready, 1)
            act.wait_ge(pads, 1)
            for c in range(LK):
                act.wait_ge(unit_done, 8 + c + 1)
                act.wait_ge(tile_drained, 8 + c)
                act.copy(xpad[:, c, 2:2 + T], bank(c)).then_inc(tile_drained, 1)
            act.wait_ge(vec_in, 16)
            for c in range(LK):
                act.wait_ge(unit_done, 12 + c + 1)
                act.wait_ge(tile_drained, 12 + c)
                act.activation(gelug[:, c, :], bank(c), ACT.Gelu_apprx_tanh).then_inc(tile_drained, 1)
            for c in range(LK):
                for g in range(4):
                    act.wait_ge(gates_ready, 4 * c + g + 1)
                    d = g // 2
                    dst, bias = (igate, "b_ig") if g % 2 else (rgate, "b_rg")
                    if c == 0 and g == 0:
                        act.wait_ge(rows_stored, 16)
                    act.activation(dst[:, d, c, :], bank(4 + g), ACT.Sigmoid,
                                   bias=col(bias, LK * d + c)).then_inc(gates_read, 1)
            act.wait_ge(lam_c, 1)
            act.wait_ge(gates_read, 4 * LK)
            for d in range(2):
                for c in range(LK):
                    act.activation(tanh_la[:, d, c, :], rgate[:, d, c, :], ACT.Tanh,
                                   scale=lamw[:, 5, LK * d + c:LK * d + c + 1]).then_inc(act_step, 1)
            for d in range(2):
                for c in range(LK):
                    act.wait_ge(act_step, LK * d + c + 1)
                    act.activation(rgate[:, d, c, :], rgate[:, d, c, :], ACT.Exp,
                                   scale=lamw[:, 5, LK * d + c:LK * d + c + 1]).then_inc(a_ready, 1)
            for d in range(2):
                act.wait_ge(w_ready, d + 1)
                act.activation(wrk[:, d], wrk[:, d], ACT.Sqrt).then_inc(root_ready, 1)
            for c in range(LK):
                act.wait_ge(cen_ready, c + 1)
                if c == 0:
                    act.wait_ge(ms_ready, 1)
                act.activation(sq[:, c, :], cacc[:, c, :], ACT.Square).then_inc(censq_ready, 1)
            for c in range(LK):
                act.wait_ge(var_ready, c + 1)
                act.activation(group_std(c), bank(4 + c), ACT.Sqrt, bias=eps).then_inc(cstd_ready, 1)
            for c in range(LK):
                act.wait_ge(cn_ready, c + 1)
                act.activation(cacc[:, c, :], cacc[:, c, :], ACT.Silu, scale=col("conf_g", c),
                               bias=col("conf_nb", c)).then_inc(yconv_ready, 1)
            norm_squares(act, "conv", [cacc[:, c, :] for c in range(LK)], lambda k: act.wait_ge(yconv_ready, k + 1))
            norm_root(act, "conv")
            norm_squares(act, "lru", [gelug[:, c, :] for c in range(LK)],
                         lambda k: act.wait_ge(ylru_ready, 1))
            act.wait_ge(n_ready, norm_tiles["conv"] + 1)
            norm_root(act, "lru")
            peer_act(act)
            layer_a_act(act)
            swiglu_act(act, "a")
            layer_b_act(act)
            swiglu_act(act, "b")
            norm_squares(act, "fin2", hs, residual_ready(act, "b_down"))
            norm_root(act, "fin2")

        @block.vector
        def _(dve):
            step = Steps(dve, dve_step)
            dve.memset(relb[NBUCKET:NBUCKET + 1, :], NEG).then_inc(rel_neg, 1)
            dve.memset(held[:, :], 0.0).then_inc(gw_zero, 1)
            dve.memset(gw, 0.0).then_inc(gw_zero, 1)
            step.do(dve.memset(xpad[:, :, 0:2], 0.0))
            step.do(dve.memset(xpad[:, :, 2 + T:], 0.0))
            step.do(dve.memset(gpad[:, :, 0:CONF_TAPS // 2], 0.0))
            step.do(dve.memset(gpad[:, :, CONF_TAPS // 2 + T:], 0.0))
            step.settle()
            dve.memset(lamw[:, 4, :], 0.0).then_inc(pads, 1)
            dve.wait_ge(vec_in, 16)
            lam = vec[:, VEC["lam"]:VEC["lam"] + 2 * LK]
            dve.scalar_tensor_tensor(out=lamw[:, 0, :], in0=lam, scalar=-1.0, in1=lam, op0=ALU.mult, op1=ALU.max).then_inc(lam_in, 1)
            norm_scale(dve, step, "mix", hs, "mix_g", ns)
            dve.wait_ge(lam_e, 1)
            dve.tensor_scalar(lamw[:, 2, :], lamw[:, 1, :], 1.0, None, ALU.add).then_inc(lam_u, 1)
            dve.wait_ge(lam_u, 1)
            step.do(dve.tensor_scalar(lamw[:, 4, :], lamw[:, 2, :], 1.0, None, ALU.subtract))
            step.settle()
            step.do(dve.tensor_scalar(lamw[:, 0, :], lamw[:, 4, :], 0.0, None, ALU.is_equal))
            step.settle()
            dve.wait_ge(lam_ln, 1)
            step.do(dve.tensor_tensor(lamw[:, 3, :], lamw[:, 3, :], lamw[:, 0, :], ALU.add))
            step.do(dve.tensor_tensor(lamw[:, 4, :], lamw[:, 4, :], lamw[:, 0, :], ALU.add))
            step.settle()
            step.do(dve.reciprocal(lamw[:, 4, :], lamw[:, 4, :]))
            step.do(dve.tensor_tensor(lamw[:, 3, :], lamw[:, 3, :], lamw[:, 1, :], ALU.mult))
            step.do(dve.tensor_scalar(lamw[:, 0, :], lam, 0.0, 8.0, ALU.min, ALU.mult))
            step.settle()
            step.do(dve.tensor_tensor(lamw[:, 3, :], lamw[:, 3, :], lamw[:, 4, :], ALU.mult))
            step.settle()
            dve.scalar_tensor_tensor(out=lamw[:, 5, :], in0=lamw[:, 3, :], scalar=-8.0, in1=lamw[:, 0, :],
                                     op0=ALU.mult, op1=ALU.add).then_inc(lam_c, 1)
            for pair in range(2):
                for c in (2 * pair, 2 * pair + 1):
                    dve.wait_ge(sigb_ready, c + 1)
                    dve.tensor_tensor(gpad[:, c, CONF_TAPS // 2:CONF_TAPS // 2 + T], bank((2 * c) % 4), sigb[:, c, :],
                                      ALU.mult).then_inc(tile_drained, 2)
                dve.wait_ge(tile_drained, 4 * pair + 4)
                for c in (2 * pair, 2 * pair + 1):
                    step.do(dve.tensor_scalar(cacc[:, c, :], gpad[:, c, 0:T], col("conf_w", c), col("conf_b", c),
                                              ALU.mult, ALU.add))
                with step.loop(1, CONF_TAPS, 2) as tap:
                    for c in (2 * pair, 2 * pair + 1):
                        step.eng.wait_ge(step.sem, step.base - 1 + c % 2)
                        step.do(dve.scalar_tensor_tensor(
                            out=cacc[:, c, :], in0=gpad[:, c, bass.ds(tap, T)],
                            scalar=vec[:, bass.ds(VEC["conf_w"] + LK * tap + c, 1)], in1=cacc[:, c, :],
                            op0=ALU.mult, op1=ALU.add))
                step.settle()
                for c in (2 * pair, 2 * pair + 1):
                    dve.engine_nop().then_inc(conv_ready, 1)
            before = step.k
            for c in range(LK):
                dve.wait_ge(tile_drained, 8 + c + 1)
                step.do(dve.tensor_scalar(xc[:, c, :], xpad[:, c, 0:T], col("lru_w", c), col("lru_b", c),
                                          ALU.mult, ALU.add))
            for tap in range(1, LRU_TAPS):
                for c in range(LK):
                    dve.wait_ge(dve_step, step.base + before + LK * (tap - 1) + c + 1)
                    ins = dve.scalar_tensor_tensor(out=xc[:, c, :], in0=xpad[:, c, tap:tap + T],
                                                   scalar=col("lru_w", LK * tap + c), in1=xc[:, c, :],
                                                   op0=ALU.mult, op1=ALU.add)
                    if tap < LRU_TAPS - 1:
                        step.do(ins)
                    else:
                        ins.then_inc(xc_ready, 1)
            for c in range(LK):
                dve.wait_ge(mean_ready, c + 1)
                dve.tensor_tensor(cacc[:, c, :], cacc[:, c, :], bank(4 + c), ALU.subtract).then_inc(cen_ready, 1)
            for d in range(2):
                dve.wait_ge(a_ready, LK * (d + 1))
                dve.wait_ge(gates_read, 4 * LK)
                step.do(dve.tensor_scalar(wrk[:, d], tanh_la[:, d], -1.0, 1.0, ALU.mult, ALU.add))
                step.do(dve.tensor_tensor(igate[:, d], igate[:, d], xc, ALU.mult))
                step.settle()
                step.do(dve.reciprocal(wrk[:, d], wrk[:, d]))
                step.settle()
                dve.scalar_tensor_tensor(out=wrk[:, d], in0=tanh_la[:, d], scalar=-2.0, in1=wrk[:, d],
                                         op0=ALU.mult, op1=ALU.mult).then_inc(w_ready, 1)
            for d in range(2):
                dve.wait_ge(root_ready, d + 1)
                step.do(dve.tensor_tensor(igate[:, d], igate[:, d], wrk[:, d], ALU.mult))
                step.settle()
                for c in range(LK):
                    order = slice(None, None, -1) if d else slice(None)
                    step.do(dve.tensor_tensor_scan(tanh_la[:, d, c, order], rgate[:, d, c, order],
                                                   igate[:, d, c, order], 0.0, ALU.mult, ALU.add))
            step.settle()
            step.do(dve.tensor_tensor(tanh_la[:, 0], tanh_la[:, 0], tanh_la[:, 1], ALU.add))
            step.settle()
            dve.tensor_tensor(gelug, gelug, tanh_la[:, 0], ALU.mult).then_inc(ylru_ready, 1)
            for c in range(LK):
                dve.wait_ge(cstd_ready, c + 1)
                step.do(dve.reciprocal(sigb[:, c, :], group_std(c)))
                step.settle()
                dve.tensor_tensor(cacc[:, c, :], cacc[:, c, :], sigb[:, c, :], ALU.mult).then_inc(cn_ready, 1)
            dve.wait_ge(unit_done, 16)
            norm_scale(dve, step, "conv", [cacc[:, c, :] for c in range(LK)], "beta_conv", ns[LK:])
            dve.wait_ge(n_ready, norm_tiles["lru"])
            norm_scale(dve, step, "lru", [gelug[:, c, :] for c in range(LK)], "beta_lru", ns[:LK])
            add_residual(dve, "w_out")
            peer_dve(dve, step)
            layer_a_dve(dve, step)
            swiglu_dve(dve, step, "a")
            layer_b_dve(dve, step)
            swiglu_dve(dve, step, "b")
            norm_scale(dve, step, "fin2", hs, "fin2_g", ns)

        @block.gpsimd
        def _(pool):
            pool.wait_ge(gw_zero, 2)
            for half in range(2):
                pool.dma_start(gw[64 * half:64 * half + 64, :, 64 * half:64 * half + 64],
                               t["gw"][half]).then_inc(gw_in, 16)
            pool.dma_start(gate_bias[:, :], t["gate_bias"].partition_broadcast(P)).then_inc(gb_in, 16)
            peer_pool(pool)
            layer_a_pool(pool)
            layer_b_pool(pool)


def units(w, order=None):
    w = np.asarray(w)
    k, o = w.shape[0] // P, w.shape[1] // P
    u = w.reshape(k, P, o, P).transpose(2, 1, 0, 3).reshape(o, P, k * P)
    return np.ascontiguousarray(u if order is None else u[list(order)])


def columns(v):
    return np.asarray(v).reshape(-1, P).T


def paired(w, axis):
    w = np.moveaxis(np.asarray(w), axis, 0)
    w = w.reshape(2, 2, GR, DH, *w.shape[1:])
    w = w.transpose(0, 2, 1, 3, *range(4, w.ndim)).reshape(NH * DH, *w.shape[4:])
    return np.moveaxis(w, 0, axis)


def t5_bucket(d):
    large = 16 + (np.log(np.maximum(d, 16).astype(np.float32) / np.float32(16)).astype(np.float32)
                  / np.float32(np.log(2048 / 16)) * np.float32(16)).astype(np.int32)
    return np.where(d < 16, d, np.minimum(large, NBUCKET - 1))


def bias_onehot():
    out = np.zeros((NBUCKET + 1, ROWLEN), np.float32)

    def put(at, d, ok):
        d, ok = np.asarray(d), np.asarray(ok)
        cols = at + np.arange(len(d))
        out[t5_bucket(np.maximum(d, 0))[ok], cols[ok]] = 1.0
        out[NBUCKET, cols[~ok]] = 1.0

    for name, (top, size, allowed) in ROWS.items():
        d = top - np.arange(size)
        put(ROW_AT[name], d, allowed(d))
    for b in range(16):
        d = (15 - b) - 31 + 16 * (31 - np.arange(CMP_LEN))
        put(ROW_AT["cmp"] + b * CMP_LEN, d, d >= 0)
    return out


def constants():
    c = np.zeros((P, NCONST), np.float32)
    c[:, 0:P] = np.eye(P)
    c[:, P:2 * P] = 1.0 / D
    c[:, 2 * P:3 * P] = 1.0 / DL
    group = np.arange(P) // 64
    c[:, 3 * P:4 * P] = (group[:, None] == group[None, :]) / 64.0
    c[:, 4 * P:4 * P + TOPK] = np.arange(TOPK)
    c[:, 4 * P + TOPK] = EPS
    c[:, 4 * P + TOPK + 1:] = np.eye(P)[::-1]
    return c


def layout(i):
    g = {k: np.asarray(v) for k, v in i.items()}
    vec = [g["mix_norm_g"][0], g["lru_conv_w"][0], g["lru_conv_b"][0], g["lru_b_rg"][0], g["lru_b_ig"][0],
           g["lru_lambda"][0], g["conf_conv_w"][0], g["conf_conv_b"][0], g["conf_norm_g"][0], g["conf_norm_b"][0],
           g["beta_lru"][0], g["beta_conv"][0], g["ffn_norm_g"][0], g["final_norm_g"], g["norm_mix_2"][0],
           g["norm_mix_2"][1], g["norm_ffn_2"][0], g["norm_ffn_2"][1], g["kv_norm_2"], g["final_norm_2"]]
    gw = np.stack([g["lru_w_rg"][0], g["lru_w_ig"][0]], 1).reshape(2, 2, LK, 2, 64, 64)
    gw = gw.transpose(3, 4, 0, 1, 2, 5).reshape(2, 64, 4 * LK, 64)
    a_in = g["a_w_in_2"][0]
    pairs = [x for c in range(LK) for x in (8 + c, 12 + c)]
    up = [x for c in range(FK) for x in (c, FK + c)]

    def down(w):
        return np.ascontiguousarray(np.asarray(w).reshape(2, 11, P, DK, P).transpose(3, 0, 2, 1, 4)
                                    .reshape(2 * DK, P, 11 * P))

    qw = g["b_w_q_2"][0]
    bq = np.concatenate([paired(qw[:, d * D:(d + 1) * D], 1) for d in range(3)], 1)
    kvw = g["kv_w_2"].reshape(D, 3, 2, 256).transpose(0, 2, 1, 3).reshape(D, 1536)
    return {
        "x": np.ascontiguousarray(g["x"][0].reshape(T, DK, P).transpose(2, 1, 0)),
        "consts": constants(), "onehot": bias_onehot(), "rel_bias_2": g["rel_bias_2"],
        "vec": np.ascontiguousarray(np.concatenate([columns(v) for v in vec], 1)),
        "gw": np.ascontiguousarray(gw), "gate_bias": np.ascontiguousarray(g["a_b_gate_2"][0]),
        "w_in": units(g["w_in"][0], pairs + list(range(8))),
        "w_out": units(g["w_out"][0]),
        "w_q": units(g["peer_w_q"][0]),
        "sub_keys": np.ascontiguousarray(g["peer_sub_keys"][0].transpose(3, 0, 1, 2).reshape(P, HP, NKEY)),
        "peer_u": g["peer_u"][0], "peer_v": g["peer_v"][0],
        "a_in": units(np.concatenate([paired(a_in[:, :D], 1), a_in[:, D:D + 1536]], 1)),
        "a_gate": np.ascontiguousarray(a_in[:, D + 1536:].reshape(DK, P, 3 * NH).transpose(1, 0, 2)),
        "pe": np.ascontiguousarray(np.stack([np.tile(g["a_pe_k_2"][0].T, (2, 1)), np.tile(g["a_pe_v_2"][0].T, (2, 1))], 1)),
        "w1": np.ascontiguousarray(np.stack([g["a_w1_k_2"][0], g["a_w1_v_2"][0]]).reshape(2, CMP_POS, DH, 256)
                                   .transpose(2, 0, 1, 3)),
        "w2": np.ascontiguousarray(np.stack([g["a_w2_k_2"][0], g["a_w2_v_2"][0]]).reshape(2, 2, P, DH)
                                   .transpose(2, 0, 1, 3)),
        "a_out": units(paired(g["a_w_out_2"][0], 0)),
        "a_up": units(g["ffn_w_up_2"][0], up), "a_down": down(g["ffn_w_down_2"][0]),
        "kv": units(kvw), "b_q": units(bq), "b_out": units(paired(g["b_w_out_2"][0], 0)),
        "b_up": units(g["ffn_w_up_2"][1], up), "b_down": down(g["ffn_w_down_2"][1]),
    }


def kernel(**inputs):
    import concourse.bacc as bacc
    from concourse.bass_utils import run_bass_kernel_spmd

    nc = bacc.Bacc("TRN2", target_bir_lowering=False, num_devices=1)
    arrays, aps = {}, {}
    for name, a in layout(inputs).items():
        arrays[f"in_{name}"] = a
        aps[name] = nc.dram_tensor(f"in_{name}", a.shape, mybir.dt.from_np(a.dtype), kind="ExternalInput").ap()
    aps["out"] = nc.dram_tensor("out_dram", (P, DK, T), F32, kind="ExternalOutput").ap()
    program(nc, aps)
    r = run_bass_kernel_spmd(nc, [arrays], core_ids=[0])
    out = r.results[0]["out_dram"]
    return np.ascontiguousarray(out.transpose(2, 1, 0)).reshape(1, T, D)
```

```python
from contextlib import ExitStack

import numpy as np

import concourse.bass as bass
from concourse import mybir

P = 128
ALU = mybir.AluOpType
ACT = mybir.ActivationFunctionType
F32 = mybir.dt.float32
F32R = mybir.dt.float32r
I32 = mybir.dt.int32
U32 = mybir.dt.uint32
AX_X = mybir.AxisListType.X

T = 512
TT = T // P
D = 1024
DK = D // P
DL = 512
LK = DL // P
LRU_TAPS, CONF_TAPS = 4, 31
EPS = 1e-6

PH, NKEY, TOPK = 8, 128, 16
SLOTS = PH * TOPK
HP = 2 * PH

NH, DH, NKV = 16, 64, 4
GR = NH // NKV
FK = 2816 // P
NBUCKET = 32
NCMP = (T - 32) // 16 + 1
CMP_POS = 32
NEG = -1e30
FLOOR = -1e29

ROWS = {
    "sel": (511, 639, lambda d: d >= 0),
    "win": (383, 511, lambda d: (d >= 0) & (d <= 255)),
    "dil0": (255, 383, lambda d: (d >= 0) & (d <= 128)),
    "dil1": (511, 639, lambda d: (d >= 0) & (d % 4 == 0)),
    "dil2": (511, 639, lambda d: (d >= 0) & (d % 16 == 0)),
}
CMP_LEN, CMP_COLS = 62, 55
ROW_AT = {}
_at = 0
for _name, (_top, _n, _ok) in ROWS.items():
    ROW_AT[_name] = _at
    _at += _n
ROW_AT["cmp"] = _at
ROWLEN = _at + 16 * CMP_LEN

VEC = {}
_at = 0
for _name, _n in (("mix_g", DK), ("lru_w", LRU_TAPS * LK), ("lru_b", LK), ("b_rg", 2 * LK), ("b_ig", 2 * LK),
                  ("lam", 2 * LK), ("conf_w", CONF_TAPS * LK), ("conf_b", LK), ("conf_g", LK), ("conf_nb", LK),
                  ("beta_lru", LK), ("beta_conv", LK), ("ffn_g", DK), ("fin1_g", DK), ("a_mix_g", DK),
                  ("b_mix_g", DK), ("a_ffn_g", DK), ("b_ffn_g", DK), ("kv_g", DK), ("fin2_g", DK)):
    VEC[_name] = _at
    _at += _n
NVEC = _at

RING = 4
STREAM = (("w_in", 16, DK), ("w_out", 8, DK), ("w_q", 16, DK), ("a_in", 20, DK), ("a_out", 8, DK),
          ("a_up", 44, DK), ("a_down", 16, 11), ("kv", 12, DK), ("b_q", 24, DK), ("b_out", 8, DK),
          ("b_up", 44, DK), ("b_down", 16, 11))
FIRST_UNIT, FIRST_TILE = {}, {}
_u = _o = 0
for _name, _n, _k in STREAM:
    FIRST_UNIT[_name], FIRST_TILE[_name] = _u, _o
    _u += _n
    _o += _n // 2 if _k == 11 else _n
ARENA = 32000
PAIR = 2
GROUPS = TOPK // PAIR
ROWRING = 4
NROWCHUNK = -(-ROWLEN // 512)
NCONST = 5 * P + TOPK + 1
NORMS = (("mix", DK), ("conv", LK), ("lru", LK), ("ffn", DK), ("fin1", DK), ("a_mix", DK), ("a_ffn", DK),
         ("kv", DK), ("b_mix", DK), ("b_ffn", DK), ("fin2", DK))
STATS = [x for x, _ in NORMS if x != "b_mix"]
NORM_TILES = sum(x for _, x in NORMS)
SPLIT = (("a_in", "a_mix"), ("a_up", "a_ffn"), ("a_down", None), ("kv", "kv"), ("b_q", "b_mix"),
         ("b_up", "b_ffn"), ("b_down", None))


def spread(ap, n):
    return ap.unsqueeze(len(ap.shape)).broadcast_to(list(ap.shape) + [n])


class Steps:

    def __init__(self, eng, sem):
        self.eng, self.sem, self.base, self.k = eng, sem, 0, 0

    def do(self, ins):
        ins.then_inc(self.sem, 1)
        self.k += 1

    def settle(self, apart=None):
        self.eng.wait_ge(self.sem, self.base + self.k)
        if apart:
            apart(self.eng)

    def loop(self, start, end, per):
        return StepLoop(self, start, end, per)


class StepLoop:
    def __init__(self, steps, start, end, per):
        self.s, self.start, self.end, self.per = steps, start, end, per

    def __enter__(self):
        self.before = self.s.base, self.s.k
        self.fori = self.s.eng.Fori(self.start, self.end)
        i = self.fori.__enter__()
        self.s.base, self.s.k = self.before[0] + self.before[1] + (i - self.start) * self.per, 0
        return i

    def __exit__(self, *exc):
        assert exc[0] or self.s.k == self.per, (self.s.k, self.per)
        self.fori.__exit__(*exc)
        self.s.base, self.s.k = self.before[0], self.before[1] + (self.end - self.start) * self.per


def program(nc, t):
    with ExitStack() as ctx:
        def sb(name, shape, dtype=F32):
            return ctx.enter_context(nc.sbuf_tensor(name, shape, dtype))

        def sem(name):
            return ctx.enter_context(nc.semaphore(name))

        ps = ctx.enter_context(nc.psum_tensor("ps", [P, 8, 512], F32))
        h = sb("h", [P, DK, T])
        n_at = nc.sbuf_base
        n = sb("n", [P, DK, T])
        sq_at = nc.sbuf_base
        sq = sb("sq", [P, DK, T])
        rstd = sb("rstd", [P, T])
        std = sb("std", [P, T])
        ring = sb("ring", [P, RING, 11 * P])
        vec = sb("vec", [P, NVEC])
        consts = sb("consts", [P, NCONST])
        held = sb("held", [P, 7])
        gate_bias = sb("gate_bias", [P, 3 * NH])
        tcmp = sb("tcmp", [P, NH, CMP_COLS])
        arena_at = nc.sbuf_base
        arena = sb("arena", [P, ARENA])
        rows_dram = nc.dram_tensor("bias_rows", (NH, ROWLEN), F32).ap()

        ident = consts[:, 0:P]
        ones_d = consts[:, P:2 * P]
        ones_l = consts[:, 2 * P:3 * P]
        ones_g = consts[:, 3 * P:4 * P]
        iota16 = consts[:, 4 * P:4 * P + TOPK]
        eps = consts[:, 4 * P + TOPK:4 * P + TOPK + 1]
        flip = consts[:, 4 * P + TOPK + 1:]

        class Region:

            def __init__(self, at=0):
                self.at = at

            def take(self, *shape):
                size = int(np.prod(shape))
                ap = arena[:, self.at:self.at + size]
                self.at += size
                assert self.at <= ARENA, self.at
                names = "abcd"[:len(shape)]
                if len(shape) > 1:
                    ap = ap.rearrange(f"p ({' '.join(names)}) -> p {' '.join(names)}",
                                      **dict(zip(names[:-1], shape[:-1])))
                return ap

        def col(name, k=0):
            return vec[:, VEC[name] + k:VEC[name] + k + 1]

        def bank(b):
            return ps[:, b, :]

        m = Region()
        xpad = m.take(LK, T + LRU_TAPS - 1)
        gpad = m.take(LK, T + CONF_TAPS - 1)
        sigb = m.take(LK, T)
        gelug = m.take(LK, T)
        xc = m.take(LK, T)
        cacc = m.take(LK, T)
        gw = m.take(4 * LK, P)
        rgate = m.take(2, LK, T)
        igate = m.take(2, LK, T)
        tanh_la = m.take(2, LK, T)
        wrk = m.take(2, LK, T)
        lamw = m.take(6, 2 * LK)
        onehot = tanh_la.rearrange("p a b c -> p (a b c)")[:, 0:ROWLEN]
        rowbuf = wrk.rearrange("p a b c -> p (a b c)")[:, 0:ROWLEN]
        relb = m.take(NH)
        e = Region()
        qT = e.take(HP, T)
        urow = qT.rearrange("p a b -> p (a b)").rearrange("p (s d) -> p s d", s=8)
        skT = e.take(HP, NKEY)
        s_all = e.take(TT, HP * NKEY)
        vrow_odd = e.take(4, D)
        vrow_even = n[:, :, :].rearrange("p a b -> p (a b)").rearrange("p (s d) -> p s d", s=4)
        vrow = [x[:, y:y + PAIR, :] for x in (vrow_even, vrow_odd) for y in (0, PAIR)]
        ntok = sq[:, :, :].rearrange("p a b -> p (a b)").rearrange("p (s d) -> p s d", s=TT)
        ncur = e.take(D)
        acc = e.take(2, D)
        scur, swork = e.take(2, NKEY), e.take(2, NKEY)
        cand, cwork = e.take(TOPK, TOPK), e.take(TOPK * TOPK)
        hot = e.take(2, TOPK, TOPK)
        topv, topi, topif = e.take(2, TOPK), e.take(2, TOPK).bitcast(U32), e.take(2, TOPK)
        bestv, pos = e.take(TOPK), e.take(TOPK).bitcast(U32)
        posab, posf = e.take(2, TOPK).bitcast(U32), e.take(2, TOPK)
        pick, ex, sm = e.take(2, TOPK), e.take(TOPK), e.take(4)
        expert_id = e.take(TT, SLOTS).bitcast(I32)
        gate = e.take(TT, SLOTS)
        idu, idv = e.take(ROWRING, PAIR).bitcast(I32), e.take(ROWRING, PAIR).bitcast(I32)
        dots, gel, wslot = e.take(ROWRING, PAIR), e.take(ROWRING, PAIR), e.take(ROWRING, PAIR)
        a = Region()
        proj = a.take(20, T)
        vtok = a.take(2, TT, 256)
        hg = a.take(2, 2, 2, 2 * NCMP)
        kcmp = a.take(2, NCMP)
        vcmp = a.take(256)
        gateA = a.take(TT, 3 * NH)
        w2 = a.take(2, 2, DH)
        pe2 = a.take(2, CMP_POS)
        wg = a.take(DK, 3 * NH)
        after = a.at
        w1 = a.take(2, CMP_POS // 2, 256)
        cin = a.take(2, NKV, NCMP * 16)
        a2 = Region(after)
        pA, ptA = a2.take(2, 1280), a2.take(2, 1280)
        tabA = a2.take(2, 896 + CMP_COLS)
        qcurA, smA = a2.take(1, T), a2.take(2, 16)
        attn = sq
        f = Region()
        silu, gated = f.take(2, T), f.take(2, T)

        def rounded(name, at, *shape):
            assert at % 32 == 0
            return nc.alloc_sbuf_tensor_at(name, [P, *shape], F32R, offset=at)

        n_hi, n_lo = rounded("n_hi", sq_at, DK, T), rounded("n_lo", n_at, DK, T)
        at = [arena_at + 4 * f.at + 4 * x for x in (0, FK * T)] + [arena_at + 4 * (ARENA - 11 * P * x) for x in (4, 2)]
        assert f.at + 2 * FK * T <= ARENA - 4 * 11 * P and a.at <= ARENA - 4 * 11 * P
        hid_hi, hid_lo = rounded("hid_hi", at[0], FK, T), rounded("hid_lo", at[1], FK, T)
        w_hi, w_lo = rounded("w_hi", at[2], 2, 11 * P), rounded("w_lo", at[3], 2, 11 * P)
        b = Region()
        qB, kvB, vtokB = b.take(24, T), b.take(12, T), b.take(3, TT, 256)
        tabB, pB, ptB = b.take(2, 1280), b.take(2, 1280), b.take(2, 1280)
        qcurB, smB = b.take(3, T), b.take(2, 16)

        x_in, vec_in, const_in, gw_in, onehot_in, rel_in = (sem(x) for x in (
            "x_in", "vec_in", "const_in", "gw_in", "onehot_in", "rel_in"))
        w_landed = [sem(f"w_landed{j}") for j in range(RING)]
        unit_done = sem("unit_done")
        tile_drained = sem("tile_drained")
        split_hi, split_lo = sem("split_hi"), sem("split_lo")
        n_split_hi, n_split_lo = sem("n_split_hi"), sem("n_split_lo")
        gated_ready, hid_hi_ready, hid_ready = sem("gated_ready"), sem("hid_hi_ready"), sem("hid_ready")
        sq_ready, ms_ready, std_ready, n_ready = sem("sq_ready"), sem("ms_ready"), sem("std_ready"), sem("n_ready")
        dve_step, act_step = sem("dve_step"), sem("act_step")
        rel_neg, row_ready, row_copied, rows_stored = sem("rel_neg"), sem("row_ready"), sem("row_copied"), sem("rows_stored")
        gw_zero, pads, gb_in = sem("gw_zero"), sem("pads"), sem("gb_in")
        sigb_ready, glu_ready, xpad_ready, gelug_ready, xc_ready = (sem(x) for x in (
            "sigb_ready", "glu_ready", "xpad_ready", "gelug_ready", "xc_ready"))
        gates_ready, gates_read, a_ready, w_ready, root_ready = (sem(x) for x in (
            "gates_ready", "gates_read", "a_ready", "w_ready", "root_ready"))
        lam_in, lam_e, lam_u, lam_ln, lam_c = (sem(x) for x in ("lam_in", "lam_e", "lam_u", "lam_ln", "lam_c"))
        ylru_ready, conv_ready, mean_ready, cen_ready, censq_ready, var_ready, cstd_ready, cn_ready, yconv_ready = (
            sem(x) for x in ("ylru_ready", "conv_ready", "mean_ready", "cen_ready", "censq_ready", "var_ready",
                             "cstd_ready", "cn_ready", "yconv_ready"))
        out_done = sem("out_done")

        def wait_tile(eng, o):
            eng.wait_ge(tile_drained, o - 3)

        def apart(dve):
            dve.tensor_copy(held[:, 0:1], held[:, 1:2])

        block = ctx.enter_context(nc.Block())

        norm_tiles = {}
        _c = 0
        for name, tiles in NORMS:
            norm_tiles[name] = _c
            _c += tiles
        squared = {name: x - (DK if name in ("b_ffn", "fin2") else 0) for name, x in norm_tiles.items()}
        norm_index = {name: i for i, name in enumerate(STATS)}

        def norm_squares(act, name, src, ready):
            for k in range(len(src)):
                ready(k)
                act.activation(sq[:, k, :], src[k], ACT.Square).then_inc(sq_ready, 1)

        def norm_root(act, name):
            act.wait_ge(ms_ready, norm_index[name] + 1)
            act.activation(std[:, :], bank(4), ACT.Sqrt, bias=eps).then_inc(std_ready, 1)

        def norm_mean(pe, name, ones):
            for k in range(dict(NORMS)[name]):
                pe.wait_ge(sq_ready, squared[name] + k + 1)
                mm = pe.matmul(bank(4), ones, sq[:, k, :], start=k == 0, stop=k == dict(NORMS)[name] - 1)
            mm.then_inc(ms_ready, 1)

        def split_rest(dve, name, k):
            dve.wait_ge(n_split_hi, split_tiles[name] + k + 1)
            dve.tensor_tensor(n_lo[:, k, :], n[:, k, :], n_hi[:, k, :], ALU.subtract).then_inc(n_split_lo, 1)

        def norm_scale(dve, step, name, src, gain, dst, again=False, split=False):
            if not again:
                dve.wait_ge(std_ready, norm_index[name] + 1)
                step.do(dve.reciprocal(rstd[:, :], std[:, :]))
                step.settle()
            for k in range(len(src)):
                dve.scalar_tensor_tensor(out=dst[k], in0=src[k], scalar=col(gain, k), in1=rstd[:, :],
                                         op0=ALU.mult, op1=ALU.mult).then_inc(n_ready, 1)
                if split and k >= 2:
                    split_rest(dve, name, k - 2)
            if split:
                for k in range(len(src) - 2, len(src)):
                    split_rest(dve, name, k)

        hs = [h[:, k, :] for k in range(DK)]
        ns = [n[:, k, :] for k in range(DK)]

        def stream(pe, name, rhs, after=None):
            _, units, kt = next(s for s in STREAM if s[0] == name)
            u0, o0 = FIRST_UNIT[name], FIRST_TILE[name]
            two = kt == 11

            def body(i, first=False):
                for j in range(RING):
                    o = o0 + 2 * i + j // 2 if two else o0 + RING * i + j
                    if two and j % 2 == 0:
                        pe.wait_ge(tile_drained, o - 1)
                    elif not two and not first:
                        wait_tile(pe, o)
                    pe.wait_ge(w_landed[j], 16 * (u0 // RING + 1 + i))
                    for k in range(kt):
                        mm = pe.matmul(bank(j // 2 if two else j), ring[:, j, k * P:(k + 1) * P],
                                       rhs[k + kt * (j % 2) if two else k],
                                       start=k == 0 and not (two and j % 2), stop=k == kt - 1 and not (two and not j % 2))
                    mm.then_inc(unit_done, 1)

            if after:
                for i in range(units // RING):
                    body(i)
                    after(i)
                return
            if u0 == 0:
                body(0, first=True)
            with pe.Fori(1 if u0 == 0 else 0, units // RING) as i:
                body(i)

        split_units, split_tiles = {}, {}
        for name, norm in SPLIT:
            split_units[name] = sum(u for x, u, _ in STREAM if x in split_units)
            if norm:
                split_tiles[norm] = DK * len(split_tiles)

        def split_rests(pool, name):
            _, units, kt = next(s for s in STREAM if s[0] == name)
            with pool.Fori(0, units // RING) as i:
                for j in range(RING):
                    pool.wait_ge(split_hi, split_units[name] + RING * i + j + 1)
                    pool.tensor_tensor(w_lo[:, j % 2, 0:kt * P], ring[:, j, 0:kt * P], w_hi[:, j % 2, 0:kt * P],
                                       ALU.subtract).then_inc(split_lo, 1)

        def act_stage(act, name, norm, *drains):
            _, units, kt = next(s for s in STREAM if s[0] == name)
            u0, rounds = FIRST_UNIT[name], units // RING

            def hi(i, no):
                j = no % RING
                act.wait_ge(w_landed[j], 16 * (u0 // RING + 1 + i + no // RING))
                act.wait_ge(unit_done, u0 + RING * i + no - 1)
                act.copy(w_hi[:, j % 2, 0:kt * P], ring[:, j, 0:kt * P]).then_inc(split_hi, 1)

            def body(i, drain, last=False):
                for j in range(RING):
                    if not last or j + 2 < RING:
                        hi(i, j + 2)
                    if drain:
                        drain(i, j)

            hi(0, 0)
            hi(0, 1)
            if norm:
                split_input(act, norm)
            ends = [x for x, _ in drains[1:]] + [rounds - 1]
            for (start, drain), end in zip(drains, ends):
                with act.Fori(start, end) as i:
                    body(i, drain)
            body(rounds - 1, drain, last=True)

        def split_input(act, norm):
            for k in range(DK):
                act.wait_ge(n_ready, norm_tiles[norm] + k + 1)
                act.copy(n_hi[:, k, :], n[:, k, :]).then_inc(n_split_hi, 1)

        def stream_split(pe, name, hi, lo):
            _, units, kt = next(s for s in STREAM if s[0] == name)
            o0, c0, two = FIRST_TILE[name], split_units[name], kt == 11
            with pe.Fori(0, units // RING) as i:
                for j in range(RING):
                    if two and j % 2 == 0:
                        pe.wait_ge(tile_drained, o0 + 2 * i + j // 2 - 1)
                    elif not two:
                        wait_tile(pe, o0 + RING * i + j)
                    pe.wait_ge(split_lo, c0 + RING * i + j + 1)
                    for k in range(kt):
                        x, cols = k + kt * (j % 2) if two else k, slice(k * P, (k + 1) * P)
                        for part, (w, r) in enumerate(((w_hi, hi), (w_hi, lo), (w_lo, hi))):
                            mm = pe.matmul(bank(j // 2 if two else j), w[:, j % 2, cols], r[:, x, :],
                                           start=k == 0 and part == 0 and not (two and j % 2),
                                           stop=k == kt - 1 and part == 2 and not (two and not j % 2))
                    mm.then_inc(unit_done, 1)

        def unit_full(eng, name, i, j):
            eng.wait_ge(unit_done, FIRST_UNIT[name] + RING * i + j + 1)

        def add_residual(dve, name):
            kt = next(s for s in STREAM if s[0] == name)[2]
            per, tiles = (2, 2) if kt == 11 else (1, RING)
            with dve.Fori(0, DK // tiles) as i:
                for j in range(tiles):
                    unit_full(dve, name, i, per * j + per - 1)
                    tile = h[:, bass.ds(tiles * i + j, 1), :].rearrange("p a t -> p (a t)")
                    dve.tensor_tensor(tile, bank(j), tile, ALU.add).then_inc(tile_drained, 1)

        def residual_ready(eng, name):
            return lambda k: eng.wait_ge(tile_drained, FIRST_TILE[name] + k + 1)

        def group_std(c):
            return sq[:, LK + c, :]

        tok_turned, tok_copied, ntok_ready, sk_in, scores_full, scores_drained = (sem(x) for x in (
            "tok_turned", "tok_copied", "ntok_ready", "sk_in", "scores_full", "scores_drained"))
        ex_ready, ex_done, ids_ready, id_copied = (sem(x) for x in ("ex_ready", "ex_done", "ids_ready", "id_copied"))
        u_landed = [sem(f"u_landed{p}") for p in range(ROWRING)]
        v_landed = [sem(f"v_landed{p}") for p in range(ROWRING)]
        dots_ready, gel_ready, v_used = sem("dots_ready"), sem("gel_ready"), sem("v_used")
        acc_ready, acc_turned, peer_added = sem("acc_ready"), sem("acc_turned"), sem("peer_added")
        ROUNDS = PH

        def group_no(tt, i, g):
            return (tt * ROUNDS + i) * GROUPS + g

        def landings(tt, i, g):
            return 16 * PAIR * ((tt * ROUNDS + i) * (GROUPS // ROWRING) + g // ROWRING + 1)

        def peer_pe(pe):
            norm_mean(pe, "ffn", ones_d)
            pe.wait_ge(n_ready, norm_tiles["ffn"] + DK)
            for q in range(2 * TT):
                if q >= 2:
                    pe.wait_ge(tok_copied, q - 1)
                for j in range(4):
                    tr = pe.transpose(ps[:, 5 + q % 2, P * j:P * j + P], n[:, 4 * (q % 2) + j, P * (q // 2):P * (q // 2) + P],
                                      ident)
                tr.then_inc(tok_turned, 1)
            pe.wait_ge(sk_in, 16)
            pe.wait_ge(tok_copied, 2 * TT)

            def scores(i):
                pe.wait_ge(tile_drained, FIRST_TILE["w_q"] + RING * (i + 1))
                for tt in range(TT):
                    if i:
                        pe.wait_ge(scores_drained, TT * (i - 1) + tt + 1)
                    for j in range(4):
                        mm = pe.matmul(ps[:, 4 + tt, P * j:P * j + P], qT[:, 4 * i + j, P * tt:P * tt + P],
                                       skT[:, 4 * i + j, :], start=True, stop=True)
                    mm.then_inc(scores_full, 1)

            stream(pe, "w_q", ns, after=scores)
            pe.wait_ge(scores_drained, 4 * TT)
            for tt in range(TT):
                pe.wait_ge(acc_ready, tt + 1)
                for q in range(2):
                    if tt:
                        pe.wait_ge(peer_added, 2 * (tt - 1) + q + 1)
                    for j in range(4):
                        tr = pe.transpose(ps[:, 5 + q, P * j:P * j + P], acc[:, 0, P * (4 * q + j):P * (4 * q + j) + P], ident)
                    tr.then_inc(acc_turned, 1)
            norm_mean(pe, "fin1", ones_d)

        def peer_act(act):
            norm_squares(act, "ffn", hs, residual_ready(act, "w_out"))
            norm_root(act, "ffn")

            def exps(i):
                act.wait_ge(ex_ready, i + 1)
                act.activation(ex, ex, ACT.Exp).then_inc(ex_done, 1)

            with act.Fori(0, HP // RING) as i:
                for j in range(RING):
                    unit_full(act, "w_q", i, j)
                    act.copy(qT[:, bass.ds(RING * i + j, 1), :], bank(j)).then_inc(tile_drained, 1)
                for tt in range(TT):
                    act.wait_ge(scores_full, TT * i + tt + 1)
                    act.copy(s_all[:, tt, bass.ds(512 * i, 512)], bank(4 + tt)).then_inc(scores_drained, 1)
                for x in range(2):
                    exps(2 * i + x)

            def gelu(w, g):
                act.wait_ge(dots_ready, GROUPS * w + g + 1)
                act.activation(gel[:, g % ROWRING, :], dots[:, g % ROWRING, :],
                               ACT.Gelu_apprx_tanh).then_inc(gel_ready, 1)

            with act.Fori(0, (TT - 1) * ROUNDS) as w:
                gelu(w, 0)
                exps(w + ROUNDS)
                for g in range(1, GROUPS):
                    gelu(w, g)
            with act.Fori((TT - 1) * ROUNDS, TT * ROUNDS) as w:
                for g in range(GROUPS):
                    gelu(w, g)
            norm_squares(act, "fin1", hs, lambda k: act.wait_ge(peer_added, 2 * TT))
            norm_root(act, "fin1")

        def retrieve(dve, step, tt, i):
            step.do(dve.tensor_copy(scur.rearrange("p a b -> p (a b)"),
                                    s_all[:, bass.ds(tt, 1), bass.ds(2 * NKEY * i, 2 * NKEY)].rearrange("p a b -> p (a b)")))
            step.settle(apart)
            for p in range(2):
                step.do(dve.max(topv[:, p, 0:8], scur[:, p, :]))
            step.settle(apart)
            for p in range(2):
                step.do(dve.max_index(topi[:, p, 0:8], topv[:, p, 0:8], scur[:, p, :]))
                step.do(dve.match_replace(swork[:, p, :], topv[:, p, 0:8], scur[:, p, :], -3e38))
            step.settle(apart)
            for p in range(2):
                step.do(dve.max(topv[:, p, 8:16], swork[:, p, :]))
            step.settle(apart)
            for p in range(2):
                step.do(dve.max_index(topi[:, p, 8:16], topv[:, p, 8:16], swork[:, p, :]))
            yield
            step.do(dve.tensor_tensor(cand, spread(topv[:, 0, :], TOPK),
                                      topv[:, 1, :].unsqueeze(1).broadcast_to([P, TOPK, TOPK]), ALU.add))
            step.settle(apart)
            flat = cand.rearrange("p a b -> p (a b)")
            step.do(dve.max(bestv[:, 0:8], flat))
            step.do(dve.tensor_copy(topif, topi))
            step.settle(apart)
            step.do(dve.max_index(pos[:, 0:8], bestv[:, 0:8], flat))
            step.do(dve.match_replace(cwork, bestv[:, 0:8], flat, -3e38))
            step.settle(apart)
            step.do(dve.max(bestv[:, 8:16], cwork))
            step.settle(apart)
            step.do(dve.max_index(pos[:, 8:16], bestv[:, 8:16], cwork))
            yield
            dve.tensor_scalar(ex, bestv, bestv[:, 0:1], None, ALU.subtract).then_inc(ex_ready, 1)
            step.settle()
            step.do(dve.tensor_scalar(posab[:, 0, :], pos, 4, None, ALU.logical_shift_right))
            step.do(dve.tensor_scalar(posab[:, 1, :], pos, 15, None, ALU.bitwise_and))
            step.settle()
            step.do(dve.tensor_copy(posf, posab))
            step.settle()
            yield
            step.do(dve.tensor_tensor(hot, spread(posf, TOPK),
                                      iota16.unsqueeze(1).unsqueeze(1).broadcast_to([P, 2, TOPK, TOPK]), ALU.is_equal))
            step.settle()
            step.do(dve.tensor_tensor(hot, hot, topif.unsqueeze(2).broadcast_to([P, 2, TOPK, TOPK]), ALU.mult))
            step.settle()
            step.do(dve.tensor_reduce(pick, hot, AX_X, ALU.add))
            step.settle()
            dve.scalar_tensor_tensor(out=expert_id[:, bass.ds(tt, 1), bass.ds(TOPK * i, TOPK)].rearrange("p a b -> p (a b)"),
                                     in0=pick[:, 0, :], scalar=float(NKEY), in1=pick[:, 1, :],
                                     op0=ALU.mult, op1=ALU.add).then_inc(ids_ready, 1)
            yield

        RETRIEVE_STEPS = 24

        def gates(dve, step, tt, i):
            dve.wait_ge(ex_done, tt * ROUNDS + i + 1)
            step.do(dve.tensor_reduce(sm[:, 0:1], ex, AX_X, ALU.add))
            step.settle()
            step.do(dve.reciprocal(sm[:, 1:2], sm[:, 0:1]))
            step.settle()
            step.do(dve.tensor_scalar(gate[:, bass.ds(tt, 1), bass.ds(TOPK * i, TOPK)].rearrange("p a b -> p (a b)"),
                                      ex, sm[:, 1:2], None, ALU.mult))
            step.settle(apart)

        GATE_STEPS = 3

        def dot_products(dve, tt, i, g):
            p = g % ROWRING
            dve.wait_ge(u_landed[p], landings(tt, i, g))
            for r in range(PAIR):
                u = urow[:, PAIR * p + r, :]
                ins = dve.tensor_tensor_reduce(out=u, in0=u, in1=ncur, scale=1.0, scalar=0.0, op0=ALU.mult, op1=ALU.add,
                                               accum_out=dots[:, p, r:r + 1])
            ins.then_inc(dots_ready, 1)

        def weighted_sum(dve, step, tt, i, g):
            p, no = g % ROWRING, group_no(tt, i, g)
            dve.wait_ge(gel_ready, no + 1)
            step.do(dve.tensor_tensor(wslot[:, p, :], gel[:, p, :],
                                      gate[:, bass.ds(tt, 1), bass.ds(TOPK * i + PAIR * g, PAIR)].rearrange("p a b -> p (a b)"),
                                      ALU.mult))
            step.settle()
            dve.wait_ge(v_used, no + 1)
            dve.wait_ge(v_landed[p], landings(tt, i, g))
            for r in range(PAIR):
                ins = dve.scalar_tensor_tensor(out=acc[:, r, :], in0=vrow[p][:, r, :], scalar=wslot[:, p, r:r + 1],
                                               in1=acc[:, r, :], op0=ALU.mult, op1=ALU.add)
            ins.then_inc(v_used, 1)

        SUM_STEPS = 1

        def peer_dve(dve, step):
            norm_scale(dve, step, "ffn", hs, "ffn_g", ns)
            for q in range(2 * TT):
                dve.wait_ge(tok_turned, q + 1)
                dve.tensor_copy(ntok[:, q // 2, 512 * (q % 2):512 * (q % 2) + 512], bank(5 + q % 2)).then_inc(tok_copied, 1)
            dve.wait_ge(scores_drained, 1)
            dve.memset(sm, 0.0).then_inc(v_used, 1)
            with step.loop(0, ROUNDS // 2, 2 * (RETRIEVE_STEPS + GATE_STEPS)) as i:
                dve.wait_ge(scores_drained, TT * i + 1)
                for x in range(2):
                    for _ in retrieve(dve, step, 0, 2 * i + x):
                        pass
                    gates(dve, step, 0, 2 * i + x)
            dve.wait_ge(scores_drained, 4 * TT)

            def tile(tt, last):
                step.do(dve.tensor_copy(ncur, ntok[:, bass.ds(tt, 1), :].rearrange("p a b -> p (a b)")))
                step.do(dve.memset(acc, 0.0))
                step.settle(apart)
                per = GROUPS * SUM_STEPS + (0 if last else RETRIEVE_STEPS + GATE_STEPS)
                with step.loop(0, ROUNDS, per) as i:
                    parts = [] if last else retrieve(dve, step, tt + 1, i)
                    for g in range(GROUPS):
                        dot_products(dve, tt, i, g)
                        if g >= 2:
                            weighted_sum(dve, step, tt, i, g - 2)
                        if g < 4 and not last:
                            next(parts)
                        if g == 6 and not last:
                            gates(dve, step, tt + 1, i)
                    weighted_sum(dve, step, tt, i, GROUPS - 2)
                    weighted_sum(dve, step, tt, i, GROUPS - 1)
                dve.wait_ge(v_used, group_no(tt, ROUNDS - 1, GROUPS - 1) + 2)
                step.settle()
                dve.tensor_tensor(acc[:, 0, :], acc[:, 0, :], acc[:, 1, :], ALU.add).then_inc(acc_ready, 1)
                for q in range(2):
                    dve.wait_ge(acc_turned, 2 * tt + q + 1)
                    part = h[:, 4 * q:4 * q + 4, bass.ds(P * tt, P)]
                    dve.tensor_tensor(part, ps[:, 5 + q, :].rearrange("p (a b) -> p a b", a=4), part,
                                      ALU.add).then_inc(peer_added, 1)
                return 2 + ROUNDS * per

            with step.loop(0, TT - 1, 2 + ROUNDS * (GROUPS * SUM_STEPS + RETRIEVE_STEPS + GATE_STEPS)) as tt:
                tile(tt, False)
            tile(TT - 1, True)
            norm_scale(dve, step, "fin1", hs, "fin1_g", hs)

        def peer_pool(pool):
            pool.wait_ge(n_ready, norm_tiles["lru"] + LK)
            pool.dma_start(skT, t["sub_keys"]).then_inc(sk_in, 16)

            def gather(tt, i, g, table, ids, rows, landed, used, least, copies):
                p = g % ROWRING
                if least is not None:
                    pool.wait_ge(used, least)
                    pool.tensor_tensor(held[:, 4:5], held[:, 1:2], held[:, 1:2], ALU.add)
                pool.tensor_copy(ids[:, p, :], expert_id[:, bass.ds(tt, 1), bass.ds(TOPK * i + PAIR * g, PAIR)]
                                 .rearrange("p a b -> p (a b)")).then_inc(id_copied, 1)
                pool.wait_ge(id_copied, copies)
                pool.tensor_tensor(held[:, 3:4], held[:, 1:2], held[:, 1:2], ALU.add)
                for r in range(PAIR):
                    pool.indirect_dma_start(rows[:, r, :], None, t[table],
                                            bass.IndirectOffsetOnAxis(ap=ids[:, p, r:r + 1], axis=0)
                                            ).then_inc(landed[p], 16)

            def round_(tt, i, first=False):
                for g in range(GROUPS):
                    p, no = g % ROWRING, group_no(tt, i, g)
                    fresh = first and g < ROWRING
                    gather(tt, i, g, "peer_u", idu, urow[:, PAIR * p:PAIR * p + PAIR, :], u_landed, dots_ready,
                           None if fresh else no - ROWRING + 1, 2 * no + 1)
                    gather(tt, i, g, "peer_v", idv, vrow[p], v_landed, v_used,
                           None if fresh else no - ROWRING + 2, 2 * no + 2)

            pool.wait_ge(scores_drained, 4 * TT)
            pool.wait_ge(ids_ready, 1)
            round_(0, 0, True)
            with pool.Fori(1, ROUNDS) as i:
                pool.wait_ge(ids_ready, i + 1)
                round_(0, i)
            with pool.Fori(1, TT) as tt:
                with pool.Fori(0, ROUNDS) as i:
                    pool.wait_ge(ids_ready, ROUNDS * tt + ROUNDS)
                    round_(tt, i)

        silu_ready = {x: sem(f"silu_ready_{x}") for x in "ab"}

        def swiglu_pe(pe, l):
            x = "ab".index(l)
            norm_mean(pe, f"{l}_ffn", ones_d)
            pe.wait_ge(n_split_lo, split_tiles[f"{l}_ffn"] + DK)
            stream_split(pe, f"{l}_up", n_hi, n_lo)
            pe.wait_ge(tile_drained, FIRST_TILE[f"{l}_up"] + 2 * FK)
            pe.wait_ge(hid_ready, FK * (x + 1))
            stream_split(pe, f"{l}_down", hid_hi, hid_lo)

        def swiglu_act(act, l):
            act.wait_ge(unit_done, FIRST_UNIT[f"{l}_out"] + DK)
            norm_squares(act, f"{l}_ffn", hs, residual_ready(act, f"{l}_out"))
            norm_root(act, f"{l}_ffn")
            o0 = FIRST_TILE[f"{l}_up"]

            def silus(i, j):
                if j % 2 == 0:
                    unit_full(act, f"{l}_up", i, j)
                    act.wait_ge(tile_drained, o0 + 4 * i + j - 2)
                    act.activation(silu[:, j // 2, :], bank(j), ACT.Silu).then_inc(silu_ready[l], 1)

            act_stage(act, f"{l}_up", f"{l}_ffn", (0, silus))
            act_stage(act, f"{l}_down", None, (0, None))

        def swiglu_dve(dve, step, l):
            x = "ab".index(l)
            norm_scale(dve, step, f"{l}_ffn", hs, f"{l}_ffn_g", ns, split=True)
            with dve.Fori(0, FK // 2) as i:
                for pr in range(2):
                    no = 2 * i + pr + 1
                    dve.wait_ge(silu_ready[l], no)
                    unit_full(dve, f"{l}_up", i, 2 * pr + 1)
                    dve.tensor_tensor(gated[:, pr, :], silu[:, pr, :], bank(2 * pr + 1), ALU.mult).then_inc(tile_drained, 2)
                    hi, lo = (y[:, bass.ds(2 * i + pr, 1), :].rearrange("p a t -> p (a t)") for y in (hid_hi, hid_lo))
                    dve.wait_ge(tile_drained, FIRST_TILE[f"{l}_up"] + 4 * i + 2 * pr + 2)
                    dve.tensor_copy(hi, gated[:, pr, :]).then_inc(hid_hi_ready, 1)
                    dve.wait_ge(hid_hi_ready, FK * x + no)
                    dve.tensor_tensor(lo, gated[:, pr, :], hi, ALU.subtract).then_inc(hid_ready, 1)
            add_residual(dve, f"{l}_down")

        def swiglu_pool(pool, l):
            split_rests(pool, f"{l}_up")
            split_rests(pool, f"{l}_down")

        class Layer:
            pass

        LA, LB = Layer(), Layer()
        LA.p, LA.pt, LA.tab, LA.q, LA.sm, LA.banks = pA, ptA, tabA, qcurA, smA, 2
        LB.p, LB.pt, LB.tab, LB.q, LB.sm, LB.banks = pB, ptB, tabB, qcurB, smB, 3
        LA.name, LB.name = "a", "b"
        for L in (LA, LB):
            (L.scores_ready, L.bank_read, L.max_ready, L.exp_done, L.probs_ready, L.turned, L.pt_copied, L.pv_done,
             L.q_staged, L.o_drained) = (sem(f"{x}_{L.name}") for x in (
                 "scores_ready", "bank_read", "max_ready", "exp_done", "probs_ready", "turned", "pt_copied", "pv_done",
                 "q_staged", "o_drained"))
            L.tab_in = [sem(f"tab_in_{L.name}{x}") for x in range(2)]
            L.tab_dmas = 3

        def branches(L, gp, half, qt):
            g, lo = 2 * gp + half, 64 * half
            rows = slice(lo, lo + 64)
            keys = P * (qt + 1)
            if L is LA:
                k0 = max(0, qt - 2)
                wide = P * (qt + 1 - k0)
                return [
                    (0, 0, keys, 0, proj[rows, 12 + gp, 0:keys], L.tab[:, half, 512 - keys:512],
                     [vtok[:, 0, x, 64 * g:64 * g + 64] for x in range(qt + 1)]),
                    (1, 0, wide, 0, proj[rows, 16 + gp, P * k0:keys], L.tab[:, half, 896 - wide:896],
                     [vtok[:, 1, x, 64 * g:64 * g + 64] for x in range(k0, qt + 1)]),
                    (1, 384, NCMP, 0, kcmp[rows, gp, :], L.tab[:, half, 896 + 24 - 8 * qt:896 + 24 - 8 * qt + NCMP],
                     [vcmp[0:NCMP, 64 * g:64 * g + 64]]),
                ]
            k0 = max(0, qt - 1)
            wide = P * (qt + 1 - k0)
            out = [(0, 0, wide, 0, kvB[rows, gp, P * k0:keys], L.tab[:, half, 256 - wide:256],
                    [vtokB[:, 0, x, 64 * g:64 * g + 64] for x in range(k0, qt + 1)])]
            for d in (1, 2):
                out.append((d, 0, keys, d, kvB[rows, 2 * d + gp, 0:keys],
                            L.tab[:, half, 256 + 512 * d - keys:256 + 512 * d],
                            [vtokB[:, d, x, 64 * g:64 * g + 64] for x in range(qt + 1)]))
            return out

        def blocks(L, gp, half, qt):
            out, at = [], 0
            for _, _, width, _, _, _, values in branches(L, gp, half, qt):
                for x, v in enumerate(values):
                    out.append((at + P * x, min(P, width - P * x), v))
                at += width
            return out

        def chunks(L, qt):
            return -(-len(blocks(L, 0, 0, qt)) // 4)

        def chunk_no(L, s):
            return sum(chunks(L, x % TT) for x in range(s))

        STEPS = 2 * TT
        OUT_CREDIT = 1
        AHEAD = 2

        def pairs(eng, pair):
            for gp in range(2):
                with eng.Fori(4 * gp, 4 * gp + 3) as it:
                    pair(it, gp, gp)
                pair(4 * gp + 3, gp, gp + 1 if gp == 0 else None)

        def slots(nxt):
            return range(AHEAD, STEPS + (AHEAD if nxt is not None else 0))

        def place(s, gp, nxt):
            half, qt = divmod(s % STEPS, TT)
            return (gp if s < STEPS else nxt), half, qt

        def attn_pe(pe, L, tiles):
            per_pair = chunk_no(L, STEPS)

            def scores(it, s, gp, nxt):
                g, half, qt = place(s, gp, nxt)
                if qt == 0:
                    pe.wait_ge(L.q_staged, 1 + tiles * (2 * it + s // TT + 1))
                seen = -1
                for bk, c, width, q, keys, _, _ in branches(L, g, half, qt):
                    use = L.banks * s + bk
                    if bk != seen and use >= 4:
                        pe.wait_ge(L.bank_read, it * (STEPS * L.banks) + use - 3)
                    pe.matmul(ps[:, use % 4, c:c + width], L.q[64 * half:64 * half + 64, q, P * qt:P * qt + P],
                              keys, start=True, stop=True).then_inc(L.scores_ready, 1)
                    seen = bk

            def turn(it, s, gp, nxt):
                g, half, qt = place(s, gp, nxt)
                pe.wait_ge(L.probs_ready, it * STEPS + s + 1)
                bl = blocks(L, g, half, qt)
                for c in range(chunks(L, qt)):
                    no = chunk_no(L, s) + c
                    if no >= 2:
                        pe.wait_ge(L.pt_copied, it * per_pair + no - 1)
                    for x, (at, width, _) in enumerate(bl[4 * c:4 * c + 4]):
                        tr = pe.transpose(ps[0:width, 4 + no % 2, P * x:P * x + P], L.p[:, s % 2, at:at + width], ident)
                    tr.then_inc(L.turned, 1)

            def values(it, s, gp, nxt):
                g, half, qt = place(s, gp, nxt)
                if qt == 0 and s:
                    pe.wait_ge(L.o_drained, OUT_CREDIT + 2 * it + s // TT - 1)
                pe.wait_ge(L.pt_copied, it * per_pair + chunk_no(L, s + 1))
                bl = blocks(L, g, half, qt)
                for x, (_, width, v) in enumerate(bl):
                    mm = pe.matmul(ps[64 * half:64 * half + 64, 6, P * qt:P * qt + P], v,
                                   L.pt[0:width, s % 2, P * x:P * x + P], start=x == 0, stop=x == len(bl) - 1)
                mm.then_inc(L.pv_done, 1)

            def pair(it, gp, nxt):
                for s in slots(nxt):
                    if s + 1 < STEPS or nxt is not None:
                        scores(it, s + 1, gp, nxt)
                    values(it, s - 1, gp, nxt)
                    turn(it, s, gp, nxt)
                if nxt is None:
                    values(it, STEPS - 1, gp, nxt)

            pe.wait_ge(L.o_drained, OUT_CREDIT)
            scores(0, 0, 0, 0)
            scores(0, 1, 0, 0)
            turn(0, 0, 0, 0)
            scores(0, 2, 0, 0)
            values(0, 0, 0, 0)
            turn(0, 1, 0, 0)
            pairs(pe, pair)

        def attn_dve(dve, step, L):
            nb = len(branches(L, 0, 0, 0))
            A = L is LA
            per_pair = chunk_no(L, STEPS)

            def row_max(it, s, gp, nxt):
                g, half, qt = place(s, gp, nxt)
                mx = L.sm[:, s % 2, 0:3]
                if qt == 0:
                    dve.wait_ge(L.tab_in[half], (it + 1 + s // STEPS) * (16 * L.tab_dmas))
                if s >= 2:
                    dve.wait_ge(L.turned, it * per_pair + chunk_no(L, s - 1))
                dve.wait_ge(L.scores_ready, it * (STEPS * nb) + nb * (s + 1))
                apart(dve)
                at = 0
                for x, (bk, c, width, _, _, tab, _) in enumerate(branches(L, g, half, qt)):
                    ins = dve.tensor_tensor_reduce(
                        out=L.p[:, s % 2, at:at + width], in0=ps[:, (L.banks * s + bk) % 4, c:c + width], in1=tab,
                        scale=1.0, scalar=FLOOR, op0=ALU.add, op1=ALU.max, accum_out=mx[:, x:x + 1])
                    at += width
                    if A and x == 1:
                        step.do(ins)
                    else:
                        ins.then_inc(L.bank_read, 1)
                dve.wait_ge(L.bank_read, it * (STEPS * L.banks) + L.banks * (s + 1))
                if A:
                    dve.tensor_scalar(L.sm[:, s % 2, 3:6], mx, -1.0, None, ALU.mult).then_inc(L.max_ready, 1)
                    return
                step.do(dve.tensor_reduce(L.sm[:, s % 2, 12:13], mx, AX_X, ALU.max))
                step.settle()
                dve.tensor_scalar(L.sm[:, s % 2, 3:4], L.sm[:, s % 2, 12:13], -1.0, None,
                                  ALU.mult).then_inc(L.max_ready, 1)

            def normalise(it, s, gp, nxt):
                g, half, qt = place(s, gp, nxt)
                dve.wait_ge(L.exp_done, it * STEPS + s + 1)
                den, inv = L.sm[:, s % 2, 6:9], L.sm[:, s % 2, 9:12]
                if A:
                    step.do(dve.tensor_scalar(inv, den, 1e-30, None, ALU.max))
                    step.settle()
                    step.do(dve.reciprocal(inv, inv))
                    step.settle()
                    g3 = gateA[:, qt, bass.ds(3 * (it + s // STEPS - 4 * g) + 3 * GR * (2 * g + half), 3)]
                    step.do(dve.tensor_tensor(inv[:, 2:3], inv[:, 2:3], g3[:, 0:1], ALU.mult))
                    step.do(dve.tensor_tensor(inv[:, 0:2], inv[:, 0:2], g3[:, 1:3], ALU.mult))
                    step.settle()
                else:
                    step.do(dve.tensor_reduce(L.sm[:, s % 2, 13:14], den, AX_X, ALU.add))
                    step.settle()
                    step.do(dve.reciprocal(inv[:, 0:1], L.sm[:, s % 2, 13:14]))
                    step.settle()
                at = 0
                br = branches(L, g, half, qt)
                if not A:
                    br = [(0, 0, sum(x[2] for x in br))]
                for x, b_ in enumerate(br):
                    pr = L.p[:, s % 2, at:at + b_[2]]
                    ins = dve.tensor_scalar(pr, pr, inv[:, x:x + 1], None, ALU.mult)
                    if x < len(br) - 1:
                        step.do(ins)
                    at += b_[2]
                ins.then_inc(L.probs_ready, 1)

            def pair(it, gp, nxt):
                for s in slots(nxt):
                    normalise(it, s, gp, nxt)
                    if s + 1 < STEPS or nxt is not None:
                        row_max(it, s + 1, gp, nxt)

            row_max(0, 0, 0, 0)
            for s in range(AHEAD):
                normalise(0, s, 0, 0)
                row_max(0, s + 1, 0, 0)
            per = STEPS * (7 if A else 3)
            for gp in range(2):
                with step.loop(4 * gp, 4 * gp + 3, per) as it:
                    pair(it, gp, gp)
                pair(4 * gp + 3, gp, gp + 1 if gp == 0 else None)

        def attn_act(act, L):
            A = L is LA
            per_pair = chunk_no(L, STEPS)

            def exponentials(it, s, gp, nxt):
                g, half, qt = place(s, gp, nxt)
                act.wait_ge(L.max_ready, it * STEPS + s + 1)
                at = 0
                for x, b_ in enumerate(branches(L, g, half, qt)):
                    pr = L.p[:, s % 2, at:at + b_[2]]
                    y = 3 + x if A else 3
                    ins = act.activation(pr, pr, ACT.Exp, bias=L.sm[:, s % 2, y:y + 1],
                                         accum_out=L.sm[:, s % 2, 6 + x:7 + x])
                    at += b_[2]
                ins.then_inc(L.exp_done, 1)

            def copy_turned(it, s, gp, nxt):
                g, half, qt = place(s, gp, nxt)
                if s >= 2:
                    act.wait_ge(L.pv_done, it * STEPS + s - 1)
                bl = blocks(L, g, half, qt)
                for c in range(chunks(L, qt)):
                    no = chunk_no(L, s) + c
                    act.wait_ge(L.turned, it * per_pair + no + 1)
                    part = bl[4 * c:4 * c + 4]
                    full = sum(w == P for _, w, _ in part)
                    src, dst = bank(4 + no % 2), L.pt[:, s % 2, 512 * c:min(512 * c + 512, 1280)]
                    if full:
                        ins = act.copy(dst[:, 0:P * full], src[:, 0:P * full])
                    if full < len(part):
                        w = part[-1][1]
                        ins = act.copy(dst[0:w, P * full:P * full + P], src[0:w, P * full:P * full + P])
                    ins.then_inc(L.pt_copied, 1)

            def drain(it, half):
                rows = slice(64 * half, 64 * half + 64)
                act.wait_ge(L.pv_done, it * STEPS + TT * (half + 1))
                act.copy(attn[rows, bass.ds(it, 1), :].rearrange("p o (a t) -> p (o a) t", a=TT),
                         bank(6)[rows].rearrange("p (a t) -> p a t", a=TT)[:, :, ::-1]).then_inc(L.o_drained, 1)

            def pair(it, gp, nxt):
                for s in slots(nxt):
                    if s + 1 < STEPS or nxt is not None:
                        exponentials(it, s + 1, gp, nxt)
                    copy_turned(it, s, gp, nxt)
                    if s == TT + 2:
                        drain(it, 0)
                drain(it, 1)

            act.copy(held[:, 2:3], held[:, 1:2]).then_inc(L.o_drained, OUT_CREDIT)
            exponentials(0, 0, 0, 0)
            for s in range(AHEAD):
                copy_turned(0, s, 0, 0)
                exponentials(0, s + 1, 0, 0)
            pairs(act, pair)

        def attn_pool(pool, L, src, tiles):
            nb = len(branches(L, 0, 0, 0))

            def stage(it, half):
                rows = slice(64 * half, 64 * half + 64)
                for d in range(tiles):
                    pool.wait_ge(L.q_staged, 1 + tiles * (2 * it + half) + d)
                    pool.tensor_copy(L.q[rows, d, :].rearrange("p (a t) -> p a t", a=TT)[:, :, ::-1],
                                     src[rows, bass.ds(8 * d + it, 1), :].rearrange("p o (a t) -> p (o a) t", a=TT)
                                     ).then_inc(L.q_staged, 1)

            mark = held[:, 5:6] if L is LA else held[:, 6:7]
            pool.tensor_tensor(mark, held[:, 1:2], held[:, 1:2], ALU.add).then_inc(L.q_staged, 1)
            stage(0, 0)
            stage(0, 1)
            with pool.Fori(1, 8) as it:
                for half in range(2):
                    pool.wait_ge(L.scores_ready, it * (STEPS * nb) + nb * (TT * (half + 1) - STEPS))
                    stage(it, half)

        def attn_tables(sp, L):
            def toeplitz(head, name, width):
                return bass.AP(tensor=rows_dram.tensor, offset=head * ROWLEN + ROW_AT[name], ap=[[1, P], [1, width]])

            for it in range(8):
                gp, r = divmod(it, GR)
                for half in range(2):
                    head = (2 * gp + half) * GR + r
                    if it:
                        sp.wait_ge(L.bank_read, ((it - 1) * STEPS + TT * (half + 1)) * L.banks)
                    if L is LA:
                        parts = [(0, 512, toeplitz(head, "sel", 512)), (512, 896, toeplitz(head, "win", 384)),
                                 (896, 896 + CMP_COLS, tcmp[:, head, :])]
                    else:
                        parts = [(0, 256, toeplitz(head, "dil0", 256)), (256, 768, toeplitz(head, "dil1", 512)),
                                 (768, 1280, toeplitz(head, "dil2", 512))]
                    for c0, c1, src in parts:
                        sp.dma_start(L.tab[:, half, c0:c1], src).then_inc(L.tab_in[half], 16)

        wg_in, w1_in, w2_in, pe_in, tcmp_in = (sem(x) for x in ("wg_in", "w1_in", "w2_in", "pe_in", "tcmp_in"))
        gl_ready, gl_biased, gate_ready, vt_turned, vt_copied, cin_ready, hc_ready, hg_ready, cmp_ready, cmp_copied = (
            sem(x) for x in ("gl_ready", "gl_biased", "gate_ready", "vt_turned", "vt_copied", "cin_ready", "hc_ready",
                             "hg_ready", "cmp_ready", "cmp_copied"))
        vt_turned_b, vt_copied_b, gate_flipped = sem("vt_turned_b"), sem("vt_copied_b"), sem("gate_flipped")

        def turn_values(pe, src, first, groups, turned, copied):
            for q in range(2 * groups):
                x, tp = divmod(q, 2)
                if q >= 2:
                    pe.wait_ge(copied, q - 1)
                for j in range(4):
                    tt, gp = 2 * tp + j // 2, j % 2
                    tr = pe.transpose(ps[:, 6 + q % 2, P * j:P * j + P], src[:, first[x] + gp, P * tt:P * tt + P], ident)
                tr.then_inc(turned, 1)

        def copy_values(dve, dst, groups, turned, copied):
            for q in range(2 * groups):
                x, tp = divmod(q, 2)
                dve.wait_ge(turned, q + 1)
                dve.tensor_copy(dst[:, x, 2 * tp:2 * tp + 2, :], bank(6 + q % 2)).then_inc(copied, 1)

        def keep(act, name, dst, scale):
            def drain(i, j):
                unit_full(act, name, i, j)
                act.mul(dst[:, bass.ds(RING * i + j, 1), :], bank(j), scale).then_inc(tile_drained, 1)
            return drain

        def layer_a_pe(pe):
            norm_mean(pe, "a_mix", ones_d)
            pe.wait_ge(n_ready, norm_tiles["a_mix"] + DK)
            pe.wait_ge(wg_in, 16)
            for tt in range(TT):
                for k in range(DK):
                    mm = pe.matmul(ps[:, 5, 48 * tt:48 * tt + 48], n[:, k, P * tt:P * tt + P], wg[:, k, :],
                                   start=k == 0, stop=k == DK - 1)
            mm.then_inc(gl_ready, 1)
            pe.wait_ge(n_split_lo, split_tiles["a_mix"] + DK)
            stream_split(pe, "a_in", n_hi, n_lo)
            pe.wait_ge(tile_drained, FIRST_TILE["a_in"] + 20)
            turn_values(pe, proj, (14, 18), 2, vt_turned, vt_copied)
            pe.wait_ge(w1_in, 16)
            for kv in range(2):
                pe.wait_ge(cin_ready, kv + 1)
                for tile in range(2):
                    for p in range(CMP_POS // 2):
                        mm = pe.matmul(ps[:, 2 * kv + tile, 0:NKV * NCMP], w1[:, kv, p, P * tile:P * tile + P],
                                       cin[:, kv, :, p:p + 16 * (NCMP - 1) + 1:16], start=p == 0,
                                       stop=p == CMP_POS // 2 - 1)
                    mm.then_inc(hc_ready, 1)
            pe.wait_ge(w2_in, 16)
            pe.wait_ge(hg_ready, 4)
            for half in range(2):
                for tile in range(2):
                    pe.matmul(ps[64 * half:64 * half + 64, 4, 0:62], w2[:, 0, tile, :], hg[:, 0, tile, half, :],
                              start=tile == 0, stop=tile == 1)
            for g in range(NKV):
                u, half = divmod(g, 2)
                for tile in range(2):
                    mm = pe.matmul(ps[0:NCMP, 5, 64 * g:64 * g + 64], hg[:, 1, tile, half, NCMP * u:NCMP * u + NCMP],
                                   w2[:, 1, tile, :], start=tile == 0, stop=tile == 1)
            mm.then_inc(cmp_ready, 1)
            pe.wait_ge(gate_ready, 1)
            pe.wait_ge(vt_copied, 4)
            pe.matmul(ps[:, 7, 0:TT * 48], flip, gateA.rearrange("p a b -> p (a b)"), start=True,
                      stop=True).then_inc(gate_flipped, 1)
            pe.wait_ge(cmp_copied, 2)
            attn_pe(pe, LA, 1)
            pe.wait_ge(LA.o_drained, OUT_CREDIT + 16)
            stream(pe, "a_out", [attn[:, k, :] for k in range(DK)])

        def layer_a_act(act):
            norm_squares(act, "a_mix", hs, lambda k: act.wait_ge(n_ready, norm_tiles["fin1"] + k + 1))
            act.wait_ge(n_ready, norm_tiles["fin1"] + DK)
            norm_root(act, "a_mix")
            act_stage(act, "a_in", "a_mix", (0, keep(act, "a_in", proj, DH ** -0.5)), (2, keep(act, "a_in", proj, 1.0)))
            act.wait_ge(gl_biased, 1)
            act.activation(gateA, gateA, ACT.Sigmoid).then_inc(gate_ready, 1)
            for kv in range(2):
                for tile in range(2):
                    act.wait_ge(hc_ready, 2 * kv + tile + 1)
                    act.activation(hg[:, kv, tile].rearrange("p a b -> p (a b)"), ps[:, 2 * kv + tile, 0:NKV * NCMP],
                                   ACT.Gelu_apprx_tanh).then_inc(hg_ready, 1)
            act.wait_ge(cmp_ready, 1)
            act.copy(kcmp, ps[:, 4, 0:62]).then_inc(cmp_copied, 1)
            act.copy(vcmp[0:NCMP, :], ps[0:NCMP, 5, 0:256]).then_inc(cmp_copied, 1)
            attn_act(act, LA)

        def layer_a_dve(dve, step):
            norm_scale(dve, step, "a_mix", hs, "a_mix_g", ns)
            dve.wait_ge(gl_ready, 1)
            for k in range(DK):
                split_rest(dve, "a_mix", k)
            dve.wait_ge(pe_in, 16)
            dve.wait_ge(tile_drained, FIRST_TILE["a_in"] + 12)
            for kv in range(2):
                for g in range(NKV):
                    rows = slice(64 * (g % 2), 64 * (g % 2) + 64)
                    for ab in range(2):
                        ins = dve.tensor_tensor(
                            cin[64 * ab:64 * ab + 64, kv, 2 * (g % 2) + g // 2, :].rearrange("p (b c) -> p b c", c=16),
                            proj[rows, 8 + 2 * kv + g // 2, 16 * ab:16 * ab + 16 * NCMP].rearrange("p (b c) -> p b c", c=16),
                            pe2[rows, kv, 16 * ab:16 * ab + 16].unsqueeze(1).broadcast_to([64, NCMP, 16]), ALU.add)
                ins.then_inc(cin_ready, 1)
            dve.wait_ge(gb_in, 16)
            dve.tensor_tensor(gateA, ps[:, 5, 0:TT * 48].rearrange("p (a b) -> p a b", a=TT),
                              gate_bias[:, :].unsqueeze(1).broadcast_to([P, TT, 48]), ALU.add).then_inc(gl_biased, 1)
            copy_values(dve, vtok, 2, vt_turned, vt_copied)
            dve.wait_ge(gate_flipped, 1)
            step.do(dve.tensor_copy(gateA.rearrange("p a b -> p (a b)"), ps[:, 7, 0:TT * 48]))
            step.settle()
            attn_dve(dve, step, LA)
            add_residual(dve, "a_out")

        def layer_a_pool(pool):
            pool.wait_ge(rows_stored, 16)
            for x in range(8):
                src = bass.AP(tensor=rows_dram.tensor, offset=ROW_AT["cmp"] + x,
                              ap=[[CMP_LEN, 16], [ROWLEN, NH], [1, CMP_COLS]])
                pool.dma_start(tcmp[16 * x:16 * x + 16, :, :], src).then_inc(tcmp_in, 16)
            pool.wait_ge(peer_added, 2 * TT)
            pool.dma_start(wg, t["a_gate"]).then_inc(wg_in, 16)
            pool.dma_start(pe2, t["pe"]).then_inc(pe_in, 16)
            pool.dma_start(w2, t["w2"]).then_inc(w2_in, 16)
            pool.dma_start(w1, t["w1"]).then_inc(w1_in, 16)
            split_rests(pool, "a_in")
            pool.wait_ge(tile_drained, FIRST_TILE["a_in"] + 8)
            pool.wait_ge(hc_ready, 4)
            attn_pool(pool, LA, proj, 1)

        def layer_a_sp(sp):
            sp.wait_ge(tcmp_in, 128)
            sp.wait_ge(hc_ready, 4)
            attn_tables(sp, LA)

        def layer_b_pe(pe):
            norm_mean(pe, "kv", ones_d)
            pe.wait_ge(n_split_lo, split_tiles["kv"] + DK)
            stream_split(pe, "kv", n_hi, n_lo)
            pe.wait_ge(tile_drained, FIRST_TILE["kv"] + 12)
            turn_values(pe, kvB, (6, 8, 10), 3, vt_turned_b, vt_copied_b)
            pe.wait_ge(n_split_lo, split_tiles["b_mix"] + DK)
            stream_split(pe, "b_q", n_hi, n_lo)
            pe.wait_ge(tile_drained, FIRST_TILE["b_q"] + 24)
            pe.wait_ge(vt_copied_b, 6)
            attn_pe(pe, LB, 3)
            pe.wait_ge(LB.o_drained, OUT_CREDIT + 16)
            stream(pe, "b_out", [attn[:, k, :] for k in range(DK)])

        def layer_b_act(act):
            norm_squares(act, "kv", hs, residual_ready(act, "a_down"))
            norm_root(act, "kv")
            act_stage(act, "kv", "kv", (0, keep(act, "kv", kvB, 1.0)))
            act_stage(act, "b_q", "b_mix", (0, keep(act, "b_q", qB, DH ** -0.5)))
            attn_act(act, LB)

        def layer_b_dve(dve, step):
            norm_scale(dve, step, "kv", hs, "kv_g", ns, split=True)
            dve.wait_ge(unit_done, FIRST_UNIT["kv"] + 12)
            norm_scale(dve, step, "b_mix", hs, "b_mix_g", ns, again=True, split=True)
            copy_values(dve, vtokB, 3, vt_turned_b, vt_copied_b)
            attn_dve(dve, step, LB)
            add_residual(dve, "b_out")

        def layer_b_pool(pool):
            split_rests(pool, "kv")
            split_rests(pool, "b_q")
            pool.wait_ge(tile_drained, FIRST_TILE["b_q"] + 24)
            attn_pool(pool, LB, qB, 3)

        def layer_b_sp(sp):
            sp.wait_ge(tile_drained, FIRST_TILE["b_down"] - 2 * FK - DK)
            attn_tables(sp, LB)

        @block.sync
        def _(sp):
            for k in range(2):
                sp.dma_start(h[:, 4 * k:4 * k + 4, :], t["x"][:, 4 * k:4 * k + 4, :]).then_inc(x_in, 16)
            sp.dma_start(consts[:, :], t["consts"]).then_inc(const_in, 16)
            sp.dma_start(vec[:, :], t["vec"]).then_inc(vec_in, 16)
            for name, units, kt in STREAM:
                u0 = FIRST_UNIT[name]
                if name == "a_out":
                    layer_a_sp(sp)
                if name == "b_out":
                    layer_b_sp(sp)

                def load(i, j, first):
                    if not first:
                        sp.wait_ge(unit_done, u0 + RING * i + j - RING + 1)
                    sp.dma_start(ring[:, j, 0:kt * P], 
                                 t[name][bass.ds(RING * i + j, 1)].rearrange("u p c -> p (u c)")).then_inc(w_landed[j], 16)

                if u0 == 0:
                    for j in range(RING):
                        load(0, j, True)
                with sp.Fori(1 if u0 == 0 else 0, units // RING) as i:
                    for j in range(RING):
                        load(i, j, False)
            sp.wait_ge(n_ready, NORM_TILES)
            sp.dma_start(t["out"], n[:, :, :]).then_inc(out_done, 16)
            sp.wait_ge(out_done, 16)

        @block.tensor
        def _(pe):
            pe.wait_ge(onehot_in, 16)
            pe.wait_ge(rel_in, 16)
            pe.wait_ge(rel_neg, 1)
            for c in range(NROWCHUNK):
                if c >= 2:
                    pe.wait_ge(row_copied, c - 1)
                w = min(512, ROWLEN - 512 * c)
                pe.matmul(ps[0:NH, 5 + c % 2, 0:w], relb[0:NBUCKET + 1, :], onehot[0:NBUCKET + 1, 512 * c:512 * c + w],
                          start=True, stop=True).then_inc(row_ready, 1)
            pe.wait_ge(const_in, 16)
            norm_mean(pe, "mix", ones_d)
            pe.wait_ge(n_ready, norm_tiles["mix"] + DK)
            stream(pe, "w_in", ns)
            pe.wait_ge(gw_in, 32)
            for c in range(LK):
                pe.wait_ge(xc_ready, c + 1)
                pe.wait_ge(row_copied, NROWCHUNK)
                for g in range(4):
                    if c >= 1:
                        pe.wait_ge(gates_read, 4 * (c - 1) + g + 1)
                    pe.matmul(bank(4 + g), gw[:, 4 * g + c, :], xc[:, c, :], start=True,
                              stop=True).then_inc(gates_ready, 1)
            for c in range(LK):
                pe.wait_ge(conv_ready, c + 1)
                if c == 0:
                    pe.wait_ge(gates_read, 4 * LK)
                pe.matmul(bank(4 + c), ones_g, cacc[:, c, :], start=True, stop=True).then_inc(mean_ready, 1)
            for c in range(LK):
                pe.wait_ge(cen_ready, c + 1)
                pe.wait_ge(censq_ready, c + 1)
                pe.matmul(bank(4 + c), ones_g, sq[:, c, :], start=True, stop=True).then_inc(var_ready, 1)
            pe.wait_ge(cstd_ready, LK)
            norm_mean(pe, "conv", ones_l)
            norm_mean(pe, "lru", ones_l)
            pe.wait_ge(n_ready, norm_tiles["lru"] + LK)
            stream(pe, "w_out", ns)
            peer_pe(pe)
            layer_a_pe(pe)
            swiglu_pe(pe, "a")
            layer_b_pe(pe)
            swiglu_pe(pe, "b")
            norm_mean(pe, "fin2", ones_d)

        @block.scalar
        def _(act):
            act.dma_start(onehot[0:NBUCKET + 1, :], t["onehot"]).then_inc(onehot_in, 16)
            act.dma_start(relb[0:NBUCKET, :], t["rel_bias_2"]).then_inc(rel_in, 16)
            act.wait_ge(const_in, 16)
            norm_squares(act, "mix", hs, lambda k: act.wait_ge(x_in, 32) if k == 0 else None)
            for c in range(NROWCHUNK):
                act.wait_ge(row_ready, c + 1)
                w = min(512, ROWLEN - 512 * c)
                act.copy(rowbuf[0:NH, 512 * c:512 * c + w], ps[0:NH, 5 + c % 2, 0:w]).then_inc(row_copied, 1)
            norm_root(act, "mix")
            act.wait_ge(row_copied, NROWCHUNK)
            act.dma_start(rows_dram, rowbuf[0:NH, :]).then_inc(rows_stored, 16)
            act.wait_ge(lam_in, 1)
            act.activation(lamw[:, 1, :], lamw[:, 0, :], ACT.Exp, scale=-1.0).then_inc(lam_e, 1)
            act.wait_ge(lam_u, 1)
            act.activation(lamw[:, 3, :], lamw[:, 2, :], ACT.Ln).then_inc(lam_ln, 1)
            for c in range(LK):
                act.wait_ge(unit_done, 2 * c + 2)
                act.activation(sigb[:, c, :], bank((2 * c + 1) % 4), ACT.Sigmoid).then_inc(sigb_ready, 1)
            act.wait_ge(pads, 1)
            for c in range(LK):
                act.wait_ge(unit_done, 8 + c + 1)
                act.wait_ge(tile_drained, 8 + c)
                act.copy(xpad[:, c, 2:2 + T], bank(c)).then_inc(tile_drained, 1)
            act.wait_ge(vec_in, 16)
            for c in range(LK):
                act.wait_ge(unit_done, 12 + c + 1)
                act.wait_ge(tile_drained, 12 + c)
                act.activation(gelug[:, c, :], bank(c), ACT.Gelu_apprx_tanh).then_inc(tile_drained, 1)
            for c in range(LK):
                for g in range(4):
                    act.wait_ge(gates_ready, 4 * c + g + 1)
                    d = g // 2
                    dst, bias = (igate, "b_ig") if g % 2 else (rgate, "b_rg")
                    if c == 0 and g == 0:
                        act.wait_ge(rows_stored, 16)
                    act.activation(dst[:, d, c, :], bank(4 + g), ACT.Sigmoid,
                                   bias=col(bias, LK * d + c)).then_inc(gates_read, 1)
            act.wait_ge(lam_c, 1)
            act.wait_ge(gates_read, 4 * LK)
            for d in range(2):
                for c in range(LK):
                    act.activation(tanh_la[:, d, c, :], rgate[:, d, c, :], ACT.Tanh,
                                   scale=lamw[:, 5, LK * d + c:LK * d + c + 1]).then_inc(act_step, 1)
            for d in range(2):
                for c in range(LK):
                    act.wait_ge(act_step, LK * d + c + 1)
                    act.activation(rgate[:, d, c, :], rgate[:, d, c, :], ACT.Exp,
                                   scale=lamw[:, 5, LK * d + c:LK * d + c + 1]).then_inc(a_ready, 1)
            for d in range(2):
                act.wait_ge(w_ready, d + 1)
                act.activation(wrk[:, d], wrk[:, d], ACT.Sqrt).then_inc(root_ready, 1)
            for c in range(LK):
                act.wait_ge(cen_ready, c + 1)
                if c == 0:
                    act.wait_ge(ms_ready, 1)
                act.activation(sq[:, c, :], cacc[:, c, :], ACT.Square).then_inc(censq_ready, 1)
            for c in range(LK):
                act.wait_ge(var_ready, c + 1)
                act.activation(group_std(c), bank(4 + c), ACT.Sqrt, bias=eps).then_inc(cstd_ready, 1)
            for c in range(LK):
                act.wait_ge(cn_ready, c + 1)
                act.activation(cacc[:, c, :], cacc[:, c, :], ACT.Silu, scale=col("conf_g", c),
                               bias=col("conf_nb", c)).then_inc(yconv_ready, 1)
            norm_squares(act, "conv", [cacc[:, c, :] for c in range(LK)], lambda k: act.wait_ge(yconv_ready, k + 1))
            norm_root(act, "conv")
            norm_squares(act, "lru", [gelug[:, c, :] for c in range(LK)],
                         lambda k: act.wait_ge(ylru_ready, 1))
            act.wait_ge(n_ready, norm_tiles["conv"] + 1)
            norm_root(act, "lru")
            peer_act(act)
            layer_a_act(act)
            swiglu_act(act, "a")
            layer_b_act(act)
            swiglu_act(act, "b")
            norm_squares(act, "fin2", hs, residual_ready(act, "b_down"))
            norm_root(act, "fin2")

        @block.vector
        def _(dve):
            step = Steps(dve, dve_step)
            dve.memset(relb[NBUCKET:NBUCKET + 1, :], NEG).then_inc(rel_neg, 1)
            dve.memset(held[:, :], 0.0).then_inc(gw_zero, 1)
            dve.memset(gw, 0.0).then_inc(gw_zero, 1)
            step.do(dve.memset(xpad[:, :, 0:2], 0.0))
            step.do(dve.memset(xpad[:, :, 2 + T:], 0.0))
            step.do(dve.memset(gpad[:, :, 0:CONF_TAPS // 2], 0.0))
            step.do(dve.memset(gpad[:, :, CONF_TAPS // 2 + T:], 0.0))
            step.settle()
            dve.memset(lamw[:, 4, :], 0.0).then_inc(pads, 1)
            dve.wait_ge(vec_in, 16)
            lam = vec[:, VEC["lam"]:VEC["lam"] + 2 * LK]
            dve.scalar_tensor_tensor(out=lamw[:, 0, :], in0=lam, scalar=-1.0, in1=lam, op0=ALU.mult, op1=ALU.max).then_inc(lam_in, 1)
            norm_scale(dve, step, "mix", hs, "mix_g", ns)
            dve.wait_ge(lam_e, 1)
            dve.tensor_scalar(lamw[:, 2, :], lamw[:, 1, :], 1.0, None, ALU.add).then_inc(lam_u, 1)
            dve.wait_ge(lam_u, 1)
            step.do(dve.tensor_scalar(lamw[:, 4, :], lamw[:, 2, :], 1.0, None, ALU.subtract))
            step.settle()
            step.do(dve.tensor_scalar(lamw[:, 0, :], lamw[:, 4, :], 0.0, None, ALU.is_equal))
            step.settle()
            dve.wait_ge(lam_ln, 1)
            step.do(dve.tensor_tensor(lamw[:, 3, :], lamw[:, 3, :], lamw[:, 0, :], ALU.add))
            step.do(dve.tensor_tensor(lamw[:, 4, :], lamw[:, 4, :], lamw[:, 0, :], ALU.add))
            step.settle()
            step.do(dve.reciprocal(lamw[:, 4, :], lamw[:, 4, :]))
            step.do(dve.tensor_tensor(lamw[:, 3, :], lamw[:, 3, :], lamw[:, 1, :], ALU.mult))
            step.do(dve.tensor_scalar(lamw[:, 0, :], lam, 0.0, 8.0, ALU.min, ALU.mult))
            step.settle()
            step.do(dve.tensor_tensor(lamw[:, 3, :], lamw[:, 3, :], lamw[:, 4, :], ALU.mult))
            step.settle()
            dve.scalar_tensor_tensor(out=lamw[:, 5, :], in0=lamw[:, 3, :], scalar=-8.0, in1=lamw[:, 0, :],
                                     op0=ALU.mult, op1=ALU.add).then_inc(lam_c, 1)
            for pair in range(2):
                for c in (2 * pair, 2 * pair + 1):
                    dve.wait_ge(sigb_ready, c + 1)
                    dve.tensor_tensor(gpad[:, c, CONF_TAPS // 2:CONF_TAPS // 2 + T], bank((2 * c) % 4), sigb[:, c, :],
                                      ALU.mult).then_inc(tile_drained, 2)
                dve.wait_ge(tile_drained, 4 * pair + 4)
                for c in (2 * pair, 2 * pair + 1):
                    step.do(dve.tensor_scalar(cacc[:, c, :], gpad[:, c, 0:T], col("conf_w", c), col("conf_b", c),
                                              ALU.mult, ALU.add))
                with step.loop(1, CONF_TAPS, 2) as tap:
                    for c in (2 * pair, 2 * pair + 1):
                        step.eng.wait_ge(step.sem, step.base - 1 + c % 2)
                        step.do(dve.scalar_tensor_tensor(
                            out=cacc[:, c, :], in0=gpad[:, c, bass.ds(tap, T)],
                            scalar=vec[:, bass.ds(VEC["conf_w"] + LK * tap + c, 1)], in1=cacc[:, c, :],
                            op0=ALU.mult, op1=ALU.add))
                step.settle()
                for c in (2 * pair, 2 * pair + 1):
                    dve.engine_nop().then_inc(conv_ready, 1)
            before = step.k
            for c in range(LK):
                dve.wait_ge(tile_drained, 8 + c + 1)
                step.do(dve.tensor_scalar(xc[:, c, :], xpad[:, c, 0:T], col("lru_w", c), col("lru_b", c),
                                          ALU.mult, ALU.add))
            for tap in range(1, LRU_TAPS):
                for c in range(LK):
                    dve.wait_ge(dve_step, step.base + before + LK * (tap - 1) + c + 1)
                    ins = dve.scalar_tensor_tensor(out=xc[:, c, :], in0=xpad[:, c, tap:tap + T],
                                                   scalar=col("lru_w", LK * tap + c), in1=xc[:, c, :],
                                                   op0=ALU.mult, op1=ALU.add)
                    if tap < LRU_TAPS - 1:
                        step.do(ins)
                    else:
                        ins.then_inc(xc_ready, 1)
            for c in range(LK):
                dve.wait_ge(mean_ready, c + 1)
                dve.tensor_tensor(cacc[:, c, :], cacc[:, c, :], bank(4 + c), ALU.subtract).then_inc(cen_ready, 1)
            for d in range(2):
                dve.wait_ge(a_ready, LK * (d + 1))
                dve.wait_ge(gates_read, 4 * LK)
                step.do(dve.tensor_scalar(wrk[:, d], tanh_la[:, d], -1.0, 1.0, ALU.mult, ALU.add))
                step.do(dve.tensor_tensor(igate[:, d], igate[:, d], xc, ALU.mult))
                step.settle()
                step.do(dve.reciprocal(wrk[:, d], wrk[:, d]))
                step.settle()
                dve.scalar_tensor_tensor(out=wrk[:, d], in0=tanh_la[:, d], scalar=-2.0, in1=wrk[:, d],
                                         op0=ALU.mult, op1=ALU.mult).then_inc(w_ready, 1)
            for d in range(2):
                dve.wait_ge(root_ready, d + 1)
                step.do(dve.tensor_tensor(igate[:, d], igate[:, d], wrk[:, d], ALU.mult))
                step.settle()
                for c in range(LK):
                    order = slice(None, None, -1) if d else slice(None)
                    step.do(dve.tensor_tensor_scan(tanh_la[:, d, c, order], rgate[:, d, c, order],
                                                   igate[:, d, c, order], 0.0, ALU.mult, ALU.add))
            step.settle()
            step.do(dve.tensor_tensor(tanh_la[:, 0], tanh_la[:, 0], tanh_la[:, 1], ALU.add))
            step.settle()
            dve.tensor_tensor(gelug, gelug, tanh_la[:, 0], ALU.mult).then_inc(ylru_ready, 1)
            for c in range(LK):
                dve.wait_ge(cstd_ready, c + 1)
                step.do(dve.reciprocal(sigb[:, c, :], group_std(c)))
                step.settle()
                dve.tensor_tensor(cacc[:, c, :], cacc[:, c, :], sigb[:, c, :], ALU.mult).then_inc(cn_ready, 1)
            dve.wait_ge(unit_done, 16)
            norm_scale(dve, step, "conv", [cacc[:, c, :] for c in range(LK)], "beta_conv", ns[LK:])
            dve.wait_ge(n_ready, norm_tiles["lru"])
            norm_scale(dve, step, "lru", [gelug[:, c, :] for c in range(LK)], "beta_lru", ns[:LK])
            add_residual(dve, "w_out")
            peer_dve(dve, step)
            layer_a_dve(dve, step)
            swiglu_dve(dve, step, "a")
            layer_b_dve(dve, step)
            swiglu_dve(dve, step, "b")
            norm_scale(dve, step, "fin2", hs, "fin2_g", ns)

        @block.gpsimd
        def _(pool):
            pool.wait_ge(gw_zero, 2)
            for half in range(2):
                pool.dma_start(gw[64 * half:64 * half + 64, :, 64 * half:64 * half + 64],
                               t["gw"][half]).then_inc(gw_in, 16)
            pool.dma_start(gate_bias[:, :], t["gate_bias"].partition_broadcast(P)).then_inc(gb_in, 16)
            peer_pool(pool)
            layer_a_pool(pool)
            swiglu_pool(pool, "a")
            layer_b_pool(pool)
            swiglu_pool(pool, "b")


def units(w, order=None):
    w = np.asarray(w)
    k, o = w.shape[0] // P, w.shape[1] // P
    u = w.reshape(k, P, o, P).transpose(2, 1, 0, 3).reshape(o, P, k * P)
    return np.ascontiguousarray(u if order is None else u[list(order)])


def columns(v):
    return np.asarray(v).reshape(-1, P).T


def paired(w, axis):
    w = np.moveaxis(np.asarray(w), axis, 0)
    w = w.reshape(2, 2, GR, DH, *w.shape[1:])
    w = w.transpose(0, 2, 1, 3, *range(4, w.ndim)).reshape(NH * DH, *w.shape[4:])
    return np.moveaxis(w, 0, axis)


def t5_bucket(d):
    large = 16 + (np.log(np.maximum(d, 16).astype(np.float32) / np.float32(16)).astype(np.float32)
                  / np.float32(np.log(2048 / 16)) * np.float32(16)).astype(np.int32)
    return np.where(d < 16, d, np.minimum(large, NBUCKET - 1))


def bias_onehot():
    out = np.zeros((NBUCKET + 1, ROWLEN), np.float32)

    def put(at, d, ok):
        d, ok = np.asarray(d), np.asarray(ok)
        cols = at + np.arange(len(d))
        out[t5_bucket(np.maximum(d, 0))[ok], cols[ok]] = 1.0
        out[NBUCKET, cols[~ok]] = 1.0

    for name, (top, size, allowed) in ROWS.items():
        d = top - np.arange(size)
        put(ROW_AT[name], d, allowed(d))
    for b in range(16):
        d = (15 - b) - 31 + 16 * (31 - np.arange(CMP_LEN))
        put(ROW_AT["cmp"] + b * CMP_LEN, d, d >= 0)
    return out


def constants():
    c = np.zeros((P, NCONST), np.float32)
    c[:, 0:P] = np.eye(P)
    c[:, P:2 * P] = 1.0 / D
    c[:, 2 * P:3 * P] = 1.0 / DL
    group = np.arange(P) // 64
    c[:, 3 * P:4 * P] = (group[:, None] == group[None, :]) / 64.0
    c[:, 4 * P:4 * P + TOPK] = np.arange(TOPK)
    c[:, 4 * P + TOPK] = EPS
    c[:, 4 * P + TOPK + 1:] = np.eye(P)[::-1]
    return c


def layout(i):
    g = {k: np.asarray(v) for k, v in i.items()}
    vec = [g["mix_norm_g"][0], g["lru_conv_w"][0], g["lru_conv_b"][0], g["lru_b_rg"][0], g["lru_b_ig"][0],
           g["lru_lambda"][0], g["conf_conv_w"][0], g["conf_conv_b"][0], g["conf_norm_g"][0], g["conf_norm_b"][0],
           g["beta_lru"][0], g["beta_conv"][0], g["ffn_norm_g"][0], g["final_norm_g"], g["norm_mix_2"][0],
           g["norm_mix_2"][1], g["norm_ffn_2"][0], g["norm_ffn_2"][1], g["kv_norm_2"], g["final_norm_2"]]
    gw = np.stack([g["lru_w_rg"][0], g["lru_w_ig"][0]], 1).reshape(2, 2, LK, 2, 64, 64)
    gw = gw.transpose(3, 4, 0, 1, 2, 5).reshape(2, 64, 4 * LK, 64)
    a_in = g["a_w_in_2"][0]
    pairs = [x for c in range(LK) for x in (8 + c, 12 + c)]
    up = [x for c in range(FK) for x in (c, FK + c)]

    def down(w):
        return np.ascontiguousarray(np.asarray(w).reshape(2, 11, P, DK, P).transpose(3, 0, 2, 1, 4)
                                    .reshape(2 * DK, P, 11 * P))

    qw = g["b_w_q_2"][0]
    bq = np.concatenate([paired(qw[:, d * D:(d + 1) * D], 1) for d in range(3)], 1)
    kvw = g["kv_w_2"].reshape(D, 3, 2, 256).transpose(0, 2, 1, 3).reshape(D, 1536)
    return {
        "x": np.ascontiguousarray(g["x"][0].reshape(T, DK, P).transpose(2, 1, 0)),
        "consts": constants(), "onehot": bias_onehot(), "rel_bias_2": g["rel_bias_2"],
        "vec": np.ascontiguousarray(np.concatenate([columns(v) for v in vec], 1)),
        "gw": np.ascontiguousarray(gw), "gate_bias": np.ascontiguousarray(g["a_b_gate_2"][0]),
        "w_in": units(g["w_in"][0], pairs + list(range(8))),
        "w_out": units(g["w_out"][0]),
        "w_q": units(g["peer_w_q"][0]),
        "sub_keys": np.ascontiguousarray(g["peer_sub_keys"][0].transpose(3, 0, 1, 2).reshape(P, HP, NKEY)),
        "peer_u": g["peer_u"][0], "peer_v": g["peer_v"][0],
        "a_in": units(np.concatenate([paired(a_in[:, :D], 1), a_in[:, D:D + 1536]], 1)),
        "a_gate": np.ascontiguousarray(a_in[:, D + 1536:].reshape(DK, P, 3 * NH).transpose(1, 0, 2)),
        "pe": np.ascontiguousarray(np.stack([np.tile(g["a_pe_k_2"][0].T, (2, 1)), np.tile(g["a_pe_v_2"][0].T, (2, 1))], 1)),
        "w1": np.ascontiguousarray(np.stack([g["a_w1_k_2"][0], g["a_w1_v_2"][0]]).reshape(2, 2, CMP_POS // 2, DH, 256)
                                   .transpose(1, 3, 0, 2, 4).reshape(P, 2, CMP_POS // 2, 256)),
        "w2": np.ascontiguousarray(np.stack([g["a_w2_k_2"][0], g["a_w2_v_2"][0]]).reshape(2, 2, P, DH)
                                   .transpose(2, 0, 1, 3)),
        "a_out": units(paired(g["a_w_out_2"][0], 0)),
        "a_up": units(g["ffn_w_up_2"][0], up), "a_down": down(g["ffn_w_down_2"][0]),
        "kv": units(kvw), "b_q": units(bq), "b_out": units(paired(g["b_w_out_2"][0], 0)),
        "b_up": units(g["ffn_w_up_2"][1], up), "b_down": down(g["ffn_w_down_2"][1]),
    }


def kernel(**inputs):
    import concourse.bacc as bacc
    from concourse.bass_utils import run_bass_kernel_spmd

    nc = bacc.Bacc("TRN2", target_bir_lowering=False, num_devices=1)
    arrays, aps = {}, {}
    for name, a in layout(inputs).items():
        arrays[f"in_{name}"] = a
        aps[name] = nc.dram_tensor(f"in_{name}", a.shape, mybir.dt.from_np(a.dtype), kind="ExternalInput").ap()
    aps["out"] = nc.dram_tensor("out_dram", (P, DK, T), F32, kind="ExternalOutput").ap()
    program(nc, aps)
    r = run_bass_kernel_spmd(nc, [arrays], core_ids=[0])
    out = r.results[0]["out_dram"]
    return np.ascontiguousarray(out.transpose(2, 1, 0)).reshape(1, T, D)
```
